# Optimizing a Trainium2 kernel written in Bass

```python
import jax, jax.numpy as jnp
from jax import lax
import numpy as np

D_MODEL = 1024
BATCH = 1
SEQ = 256
DEPTH = 2

F32 = jnp.float32
EPS = 1e-6
NEG = -1e30
FORCE = 1e9
D_MIX = D_MODEL
D_LRU = D_MIX // 4
D_ATT = D_MIX // 2
D_CONV = D_MIX - D_LRU - D_ATT
LRU_BLOCKS = 4
LRU_BW = D_LRU // LRU_BLOCKS
LRU_CONV_W = 4
LRU_C = 8.0
HEAD_DIM = 64
N_HEADS = D_ATT // HEAD_DIM
N_KV = 2
GQA = N_HEADS // N_KV
KV_W = N_KV * HEAD_DIM
ROPE_THETA = 10000.0
CMP_LEN = 32
CMP_STRIDE = 16
CMP_HID = 256
SLC_LEN = 64
SLC_TOPN = 16
WINDOW = 512
Q_BLOCK = 128
CONV_K = 31
MOE_GROUPS = 4
MOE_EXPERTS = 4
MOE_TOPK = 2
MOE_HID = 512
IN_SIZES = [D_LRU, D_LRU, D_ATT, KV_W, KV_W, KV_W, KV_W, KV_W, KV_W, 3 * N_HEADS, 2 * D_CONV]
IN_COLS = sum(IN_SIZES)

kernel_name = 'hybrid_rglru_nsa_conformer_hmoe_adaln'

def _rmsnorm(x, g):
    xf = x.astype(F32)
    y = xf * lax.rsqrt(jnp.mean(xf * xf, axis=-1, keepdims=True) + EPS)
    return (y * g.astype(F32)).astype(x.dtype)

def _layernorm(x, g, b):
    xf = x.astype(F32)
    mu = jnp.mean(xf, axis=-1, keepdims=True)
    var = jnp.mean(jnp.square(xf - mu), axis=-1, keepdims=True)
    return ((xf - mu) * lax.rsqrt(var + EPS) * g.astype(F32) + b.astype(F32)).astype(x.dtype)

def _rope_tables(positions):
    inv = ROPE_THETA ** (-jnp.arange(0, HEAD_DIM, 2, dtype=F32) / HEAD_DIM)
    ang = positions.astype(F32)[..., None] * inv
    ang = jnp.concatenate([ang, ang], axis=-1)[:, :, None, :]
    return jnp.cos(ang), jnp.sin(ang)

def _rope(x, cos, sin):
    half = x.shape[-1] // 2
    rot = jnp.concatenate([-x[..., half:], x[..., :half]], axis=-1)
    return (x * cos + rot * sin).astype(x.dtype)

def _causal_dwconv(x, w, b):
    k = w.shape[0]
    y = lax.conv_general_dilated(x, w[:, None, :].astype(x.dtype), window_strides=(1,),
                                 padding=[(k - 1, 0)], dimension_numbers=('NWC', 'WIO', 'NWC'),
                                 feature_group_count=x.shape[-1])
    return y + b

def _rglru(xl, gl, conv_w, conv_b, wa, ba, wx, bx, lam):
    B_, S_, _ = xl.shape
    xc = _causal_dwconv(xl, conv_w, conv_b)
    xb = xc.reshape(B_, S_, LRU_BLOCKS, LRU_BW)
    r = jax.nn.sigmoid(jnp.einsum('bsnd,nde->bsne', xb, wa).reshape(B_, S_, D_LRU) + ba)
    i = jax.nn.sigmoid(jnp.einsum('bsnd,nde->bsne', xb, wx).reshape(B_, S_, D_LRU) + bx)
    log_a = LRU_C * r.astype(F32) * jax.nn.log_sigmoid(lam.astype(F32))
    a = jnp.exp(log_a)
    u = jnp.sqrt(-jnp.expm1(2.0 * log_a)) * (i * xc).astype(F32)

    def combine(left, right):
        a1, b1 = left
        a2, b2 = right
        return a1 * a2, a2 * b1 + b2

    _, h = lax.associative_scan(combine, (a, u), axis=1)
    return h.astype(xl.dtype) * jax.nn.gelu(gl)

def _nsa(q, kc, vc, ks, vs, kw, vw, gate_logits, cos, sin, cmp_k_w1, cmp_k_w2, cmp_v_w1, cmp_v_w2,
         cmp_pos_k, cmp_pos_v):
    B_, S_ = q.shape[:2]
    dt = q.dtype
    q = _rope(q.reshape(B_, S_, N_HEADS, HEAD_DIM), cos, sin)
    kv_shape = (B_, S_, N_KV, HEAD_DIM)
    kc = _rope(kc.reshape(kv_shape), cos, sin)
    ks = _rope(ks.reshape(kv_shape), cos, sin)
    kw = _rope(kw.reshape(kv_shape), cos, sin)
    vc, vs, vw = vc.reshape(kv_shape), vs.reshape(kv_shape), vw.reshape(kv_shape)

    n_cmp = (S_ - CMP_LEN) // CMP_STRIDE + 1
    idx = jnp.arange(n_cmp)[:, None] * CMP_STRIDE + jnp.arange(CMP_LEN)[None, :]

    def compress(t, pos, w1, w2):
        blk = t[:, idx] + pos[None, None, :, None, :]
        blk = jnp.transpose(blk, (0, 1, 3, 2, 4)).reshape(B_, n_cmp, N_KV, CMP_LEN * HEAD_DIM)
        return jax.nn.gelu(blk @ w1) @ w2

    kcmp = compress(kc, cmp_pos_k, cmp_k_w1, cmp_k_w2)
    vcmp = compress(vc, cmp_pos_v, cmp_v_w1, cmp_v_w2)
    cmp_end = jnp.arange(n_cmp) * CMP_STRIDE + CMP_LEN - 1

    n_slc = S_ // SLC_LEN
    n_top = min(SLC_TOPN, n_slc)
    ratio = SLC_LEN // CMP_STRIDE
    pad_cmp = n_slc * ratio - n_cmp
    ks_blk = jnp.transpose(ks.reshape(B_, n_slc, SLC_LEN, N_KV, HEAD_DIM), (0, 3, 1, 2, 4))
    vs_blk = jnp.transpose(vs.reshape(B_, n_slc, SLC_LEN, N_KV, HEAD_DIM), (0, 3, 1, 2, 4))
    kw_pad = jnp.pad(kw, ((0, 0), (WINDOW, 0), (0, 0), (0, 0)))
    vw_pad = jnp.pad(vw, ((0, 0), (WINDOW, 0), (0, 0), (0, 0)))
    gates = jax.nn.sigmoid(gate_logits.astype(F32)).reshape(B_, S_, N_HEADS, 3)
    scale = HEAD_DIM ** -0.5
    bi = jnp.arange(B_)[:, None, None, None]
    ki = jnp.arange(N_KV)[None, :, None, None]
    jsl = jnp.arange(n_slc)

    def block(qb):
        s0 = qb * Q_BLOCK
        t = s0 + jnp.arange(Q_BLOCK)
        qg = lax.dynamic_slice_in_dim(q, s0, Q_BLOCK, axis=1).reshape(B_, Q_BLOCK, N_KV, GQA, HEAD_DIM) * scale
        sc = jnp.einsum('bqkgd,bnkd->bkgqn', qg, kcmp).astype(F32)
        valid_c = cmp_end[None, :] <= t[:, None]
        pc = jax.nn.softmax(jnp.where(valid_c, sc, NEG), axis=-1) * jnp.any(valid_c, axis=-1)[:, None].astype(F32)
        o_cmp = jnp.einsum('bkgqn,bnkd->bqkgd', pc.astype(dt), vcmp)
        imp = jnp.pad(pc.sum(axis=2), ((0, 0), (0, 0), (0, 0), (0, pad_cmp)))
        imp = imp.reshape(B_, N_KV, Q_BLOCK, n_slc, ratio).sum(-1)
        forced = (jsl[None, :] == 0) | (jsl[None, :] == (t // SLC_LEN)[:, None])
        causal_s = (jsl[None, :] * SLC_LEN) <= t[:, None]
        imp = jnp.where(forced, FORCE, jnp.where(causal_s, imp, -1.0))
        _, sel = lax.top_k(imp, n_top)
        ksel = ks_blk[bi, ki, sel]
        vsel = vs_blk[bi, ki, sel]
        ss = jnp.einsum('bqkgd,bkqnld->bkgqnl', qg, ksel).astype(F32).reshape(B_, N_KV, GQA, Q_BLOCK, n_top * SLC_LEN)
        pos_s = (sel[..., None] * SLC_LEN + jnp.arange(SLC_LEN)).reshape(B_, N_KV, Q_BLOCK, n_top * SLC_LEN)
        mask_s = pos_s <= t[None, None, :, None]
        ps = jax.nn.softmax(jnp.where(mask_s[:, :, None], ss, NEG), axis=-1)
        ps = ps.reshape(B_, N_KV, GQA, Q_BLOCK, n_top, SLC_LEN)
        o_slc = jnp.einsum('bkgqnl,bkqnld->bqkgd', ps.astype(dt), vsel)
        kwin = lax.dynamic_slice_in_dim(kw_pad, s0, WINDOW + Q_BLOCK, axis=1)
        vwin = lax.dynamic_slice_in_dim(vw_pad, s0, WINDOW + Q_BLOCK, axis=1)
        pos_w = s0 - WINDOW + jnp.arange(WINDOW + Q_BLOCK)
        dist = t[:, None] - pos_w[None, :]
        mask_w = (pos_w[None, :] >= 0) & (dist >= 0) & (dist < WINDOW)
        sw = jnp.einsum('bqkgd,bwkd->bkgqw', qg, kwin).astype(F32)
        pw = jax.nn.softmax(jnp.where(mask_w, sw, NEG), axis=-1)
        o_win = jnp.einsum('bkgqw,bwkd->bqkgd', pw.astype(dt), vwin)
        g = lax.dynamic_slice_in_dim(gates, s0, Q_BLOCK, axis=1).reshape(B_, Q_BLOCK, N_KV, GQA, 3)
        o = g[..., 0:1] * o_cmp + g[..., 1:2] * o_slc + g[..., 2:3] * o_win
        return o.reshape(B_, Q_BLOCK, D_ATT).astype(dt)

    out = lax.map(block, jnp.arange(S_ // Q_BLOCK))
    return jnp.transpose(out, (1, 0, 2, 3)).reshape(B_, S_, D_ATT)

def _conformer_conv(u, dw_w, dw_b, ln_g, ln_b):
    v = u[..., :D_CONV] * jax.nn.sigmoid(u[..., D_CONV:])
    v = _causal_dwconv(v, dw_w, dw_b)
    v = _layernorm(v, ln_g, ln_b)
    return jax.nn.silu(v)

def _hier_moe(h, rg_w, rg_b, re_w, re_b, w_gate, w_up, w_down):
    B_, S_, D_ = h.shape
    t = h.reshape(B_ * S_, D_)
    lg = (t @ rg_w + rg_b).astype(F32)
    pg = jax.nn.softmax(lg, axis=-1)
    g_star = jnp.argmax(lg, axis=-1)
    pg_star = jnp.take_along_axis(pg, g_star[:, None], axis=1)
    le = (jnp.einsum('td,gde->tge', t, re_w) + re_b).astype(F32)
    le_star = jnp.take_along_axis(le, g_star[:, None, None], axis=1)[:, 0]
    top_v, top_i = lax.top_k(le_star, MOE_TOPK)
    pe = jax.nn.softmax(top_v, axis=-1)
    w_e = jnp.einsum('tk,tke->te', pe, jax.nn.one_hot(top_i, MOE_EXPERTS, dtype=F32))
    comb = (jax.nn.one_hot(g_star, MOE_GROUPS, dtype=F32)[:, :, None] * w_e[:, None, :]
            * pg_star[:, :, None]).astype(t.dtype)
    y = jnp.zeros_like(t)
    for g in range(MOE_GROUPS):
        hid = jax.nn.silu(jnp.einsum('td,edf->tef', t, w_gate[g])) * jnp.einsum('td,edf->tef', t, w_up[g])
        y = y + jnp.einsum('tef,efd->td', hid * comb[:, g, :, None], w_down[g])
    return y.reshape(B_, S_, D_)

def setup_inputs(seed: int = 0) -> dict:
    key = jax.random.key(seed)
    ks = iter(jax.random.split(key, 48))
    L = DEPTH

    def nrm(shape, s):
        return jax.random.normal(next(ks), shape, F32) * s

    def gain(shape):
        return 1.0 + nrm(shape, 0.02)

    x = nrm((BATCH, SEQ, D_MODEL), 1.0)
    c = nrm((BATCH, D_MODEL), 1.0)
    start = jax.random.randint(next(ks), (BATCH, 1), 0, 1024, dtype=jnp.int32)
    positions = start + jnp.arange(SEQ, dtype=jnp.int32)[None, :]
    a0 = jax.random.uniform(next(ks), (L, D_LRU), F32, 0.9, 0.999)
    lru_lambda = jnp.log(a0) - jnp.log1p(-a0)
    return {
        'x': x, 'c': c, 'positions': positions,
        'ada_w': nrm((L, D_MODEL, 6 * D_MODEL), 0.5 * D_MODEL ** -0.5),
        'ada_b': nrm((L, 6 * D_MODEL), 0.02),
        'norm1_g': gain((L, D_MODEL)),
        'norm2_g': gain((L, D_MODEL)),
        'w_in': nrm((L, D_MODEL, IN_COLS), D_MODEL ** -0.5),
        'lru_conv_w': nrm((L, LRU_CONV_W, D_LRU), LRU_CONV_W ** -0.5),
        'lru_conv_b': nrm((L, D_LRU), 0.02),
        'lru_wa': nrm((L, LRU_BLOCKS, LRU_BW, LRU_BW), LRU_BW ** -0.5),
        'lru_ba': nrm((L, D_LRU), 0.02),
        'lru_wx': nrm((L, LRU_BLOCKS, LRU_BW, LRU_BW), LRU_BW ** -0.5),
        'lru_bx': nrm((L, D_LRU), 0.02),
        'lru_lambda': lru_lambda,
        'cmp_k_w1': nrm((L, CMP_LEN * HEAD_DIM, CMP_HID), (CMP_LEN * HEAD_DIM) ** -0.5),
        'cmp_k_w2': nrm((L, CMP_HID, HEAD_DIM), CMP_HID ** -0.5),
        'cmp_v_w1': nrm((L, CMP_LEN * HEAD_DIM, CMP_HID), (CMP_LEN * HEAD_DIM) ** -0.5),
        'cmp_v_w2': nrm((L, CMP_HID, HEAD_DIM), CMP_HID ** -0.5),
        'cmp_pos_k': nrm((L, CMP_LEN, HEAD_DIM), 0.02),
        'cmp_pos_v': nrm((L, CMP_LEN, HEAD_DIM), 0.02),
        'cnv_dw_w': nrm((L, CONV_K, D_CONV), CONV_K ** -0.5),
        'cnv_dw_b': nrm((L, D_CONV), 0.02),
        'cnv_ln_g': gain((L, D_CONV)),
        'cnv_ln_b': nrm((L, D_CONV), 0.02),
        'out_norm_g': gain((L, D_MIX)),
        'w_out': nrm((L, D_MIX, D_MODEL), D_MIX ** -0.5),
        'moe_rg_w': nrm((L, D_MODEL, MOE_GROUPS), D_MODEL ** -0.5),
        'moe_rg_b': nrm((L, MOE_GROUPS), 0.01),
        'moe_re_w': nrm((L, MOE_GROUPS, D_MODEL, MOE_EXPERTS), D_MODEL ** -0.5),
        'moe_re_b': nrm((L, MOE_GROUPS, MOE_EXPERTS), 0.01),
        'moe_w_gate': nrm((L, MOE_GROUPS, MOE_EXPERTS, D_MODEL, MOE_HID), D_MODEL ** -0.5),
        'moe_w_up': nrm((L, MOE_GROUPS, MOE_EXPERTS, D_MODEL, MOE_HID), D_MODEL ** -0.5),
        'moe_w_down': nrm((L, MOE_GROUPS, MOE_EXPERTS, MOE_HID, D_MODEL), MOE_HID ** -0.5),
        'final_norm_g': gain((D_MODEL,)),
    }

def reference(x, c, positions, ada_w, ada_b, norm1_g, norm2_g, w_in, lru_conv_w, lru_conv_b, lru_wa, lru_ba,
              lru_wx, lru_bx, lru_lambda, cmp_k_w1, cmp_k_w2, cmp_v_w1, cmp_v_w2, cmp_pos_k, cmp_pos_v,
              cnv_dw_w, cnv_dw_b, cnv_ln_g, cnv_ln_b, out_norm_g, w_out, moe_rg_w, moe_rg_b, moe_re_w,
              moe_re_b, moe_w_gate, moe_w_up, moe_w_down, final_norm_g):
    cos, sin = _rope_tables(positions)
    split_pts = [int(v) for v in np.cumsum(IN_SIZES)[:-1]]
    sc = jax.nn.silu(c)
    for l in range(DEPTH):
        mod = sc @ ada_w[l] + ada_b[l]
        sh1, sc1, g1, sh2, sc2, g2 = [m[:, None, :] for m in jnp.split(mod, 6, axis=-1)]
        h = _rmsnorm(x, norm1_g[l]) * (1.0 + sc1) + sh1
        p = h @ w_in[l]
        (xl, gl, qa, kc, vc, ksl, vsl, kwn, vwn, gate_lg, cv) = jnp.split(p, split_pts, axis=-1)
        y_lru = _rglru(xl, gl, lru_conv_w[l], lru_conv_b[l], lru_wa[l], lru_ba[l], lru_wx[l], lru_bx[l],
                       lru_lambda[l])
        y_att = _nsa(qa, kc, vc, ksl, vsl, kwn, vwn, gate_lg, cos, sin, cmp_k_w1[l], cmp_k_w2[l],
                     cmp_v_w1[l], cmp_v_w2[l], cmp_pos_k[l], cmp_pos_v[l])
        y_cnv = _conformer_conv(cv, cnv_dw_w[l], cnv_dw_b[l], cnv_ln_g[l], cnv_ln_b[l])
        gn = out_norm_g[l]
        y = jnp.concatenate([_rmsnorm(y_lru, gn[:D_LRU]),
                             _rmsnorm(y_att, gn[D_LRU:D_LRU + D_ATT]),
                             _rmsnorm(y_cnv, gn[D_LRU + D_ATT:])], axis=-1)
        x = x + g1 * (y @ w_out[l])
        h2 = _rmsnorm(x, norm2_g[l]) * (1.0 + sc2) + sh2
        x = x + g2 * _hier_moe(h2, moe_rg_w[l], moe_rg_b[l], moe_re_w[l], moe_re_b[l], moe_w_gate[l],
                               moe_w_up[l], moe_w_down[l])
    return _rmsnorm(x, final_norm_g)


_drawn_inputs = setup_inputs


def setup_inputs(seed=0):
    import zlib

    import numpy as np

    out = dict(_drawn_inputs(seed))
    spreads = {}
    factors = {'norm1_g': 4.379,
     'norm2_g': 3.266,
     'lru_conv_b': 3.784,
     'lru_ba': 8.0,
     'lru_bx': 8.0,
     'cmp_pos_k': 8.0,
     'cmp_pos_v': 6.858,
     'cnv_dw_b': 4.368,
     'cnv_ln_g': 6.47,
     'cnv_ln_b': 7.127,
     'out_norm_g': 3.778,
     'moe_rg_b': 6.68,
     'moe_re_b': 7.734,
     'final_norm_g': 2.863}
    for name, (base, spread) in spreads.items():
        noise = np.random.default_rng([zlib.crc32(name.encode()), seed]).standard_normal(out[name].shape)
        drawn = base * np.exp(spread * noise) if base else spread * noise
        out[name] = __import__('jax').numpy.asarray(drawn.astype(out[name].dtype))
    for name, factor in factors.items():
        out[name] = (out[name] * factor).astype(out[name].dtype)
    return out
```

```python
import numpy as np
import concourse.bass as bass
from concourse import mybir
from contextlib import ExitStack

P = 128
D = 1024
S = 256
TT = S // P
L = 2
KD = D // P
D_LRU, D_ATT, D_CONV = 256, 512, 256
HD, NH, NKV = 64, 8, 2
GQA = NH // NKV
CMP_LEN, CMP_STRIDE, CMP_HID = 32, 16, 256
NCMP = (S - CMP_LEN) // CMP_STRIDE + 1
LRU_W, CONV_K = 4, 31
NG, NE, FH = 4, 4, 512
EPS = 1e-6
NEG = -1e30
THETA = 10000.0
LP = CMP_LEN * HD // P
CH = 512
SLOT = 4096
NSLOT = 6
NC6 = 6 * D
IN_COLS = 2328
C_CONV, C_LRU, C_Q, C_KV, C_WIN = (1816, 2328), (0, 512), (512, 1024), (1024, 1536), (1536, 1816)


def layout(fields):
    at, out = 0, {}
    for name, n in fields:
        out[name] = (at, at + n)
        at += n
    return out, at


CONST, NCONST = layout([("ident", P), ("ones", P), ("causal", 2 * P), ("cmask", TT * NCMP), ("anyv", TT),
                        ("tri", P), ("iota", P), ("gidx", NG), ("gfar", NG), ("rot", P), ("dup", 2 * P),
                        ("rep", 2 * NH * NCMP), ("blk", NH), ("inv", 1), ("eps", 1)])
PARAM, NPARAM = layout([("n1g", KD), ("n2g", KD), ("adab", 4 * KD), ("lcw", 2 * LRU_W), ("lcb", 2), ("ba", 2),
                        ("bx", 2), ("lam", 2), ("ccw", 2 * CONV_K), ("ccb", 2), ("lng", 2), ("lnb", 2),
                        ("gn", KD), ("rb", NG + NG * NE), ("posk", LP), ("posv", LP), ("wa", 2 * P),
                        ("wx", 2 * P), ("rw", KD * (NG + NG * NE)), ("w2k", 2 * P), ("w2v", 2 * HD)])
NR = NG + NG * NE


def constants():
    c = np.zeros((P, NCONST), np.float32)

    def put(name, a, rows=P):
        lo, hi = CONST[name]
        c[:rows, lo:hi] = np.asarray(a, np.float32).reshape(rows, hi - lo)

    p = np.arange(P)
    eye = np.eye(P)
    put("ident", eye)
    put("ones", np.ones((P, P)))
    put("causal", np.concatenate([np.zeros((P, P)), np.where(p[None, :] <= p[:, None], 0.0, NEG)], 1))
    t = p[:, None] + P * np.arange(TT)[None, :]
    end = np.arange(NCMP) * CMP_STRIDE + CMP_LEN - 1
    valid = end[None, None, :] <= t[:, :, None]
    put("cmask", np.where(valid, 0.0, NEG))
    put("anyv", valid.any(-1))
    put("tri", p[:, None] < p[None, :])
    put("iota", np.tile(p + 1, (P, 1)))
    put("gidx", np.tile(np.arange(NG), (P, 1)))
    put("gfar", np.tile(np.arange(NG) + 1000, (P, 1)))
    rot = np.zeros((P, P))
    for m in range(P):
        if m % HD < HD // 2:
            rot[m + HD // 2, m] = -1
        else:
            rot[m - HD // 2, m] = 1
    put("rot", rot)
    dup = np.zeros((P, 2, P))
    for h in range(2):
        for m in range(P):
            dup[h * HD + m % HD, h, m] = 1
    put("dup", dup)
    rep = np.zeros((NCMP, 2, NH, NCMP))
    for h in range(NH):
        for n in range(NCMP):
            rep[n, h // GQA, h, n] = 1
    put("rep", rep, NCMP)
    blk = np.zeros((NH * NCMP, NH))
    for h in range(NH):
        blk[h * NCMP:(h + 1) * NCMP, h] = 1
    put("blk", blk, NH * NCMP)
    inv = np.float32(THETA) ** (-np.arange(0, HD, 2, dtype=np.float32) / np.float32(HD))
    put("inv", inv[p % (HD // 2)])
    put("eps", np.full(P, EPS))
    return c


class Waits:

    def __init__(self):
        self.n, self.turn, self.per, self.start = {}, None, {}, {}

    def __call__(self, name, by=1):
        self.n[name] = self.n.get(name, 0) + by
        return self.now(name)

    def now(self, name):
        if self.turn is None:
            return self.n[name]
        return self.turn * self.per[name] + self.n[name]

    def loop(self, turn, per):
        self.turn, self.per, self.start = turn, per, dict(self.n)

    def end(self, turns):
        for name, n in self.n.items():
            if n != self.start.get(name, 0):
                assert n - self.start.get(name, 0) == self.per[name], (name, n - self.start.get(name, 0))
                self.n[name] += (turns - 1) * self.per[name]
        self.turn = None


PASS_SEMS = ("act_full", "act_free", "dve_full", "dve_free", "dve_steps", "sel_ready", "hidT_read", "ys_ready")
TURNS = {"act_full": 1 + 2 * NE, "act_free": 1 + 2 * NE, "dve_full": 4 + NE + 4, "dve_free": 4 + NE + 4,
         "dve_steps": 2 + 4 + 1, "sel_ready": 1, "hidT_read": NE, "ys_ready": 1}
SEMS = ("consts", "c_in", "x_in", "sc_ready", "bias_row", "acc_ready", "acc_read", "modcols", "norm_root", "xn_ready",
        "conv_sum", "conv_sq", "conv_sd", "conv_ln", "conv_silu", "conv_sq2", "lru_conv", "lru_at", "lru_q",
        "lru_root", "lru_sq", "rope_ready", "gate_th", "cmp_s", "cmp_p", "s_ready", "p_ready", "pT_read",
        "o_free", "att_ss", "att_root", "att_n", "y_ready", "lg_ready", "lg_exp", "top_d", "top_exp",
        "routed", "lam_a", "lam_e", "lam_w", "lam_ln", "angle", "trig", "x_done", "act_steps", "gain_in",
        "out_ready", "stored", "pool_steps")

OWN = ("ada4", "conv", "lru", "q", "kv", "ada5", "win", "cmpk", "cmpv", "ada6", "ada7", "ada8", "ada9", "ada10",
       "ada11")
HEADS = [(("ada0", "ada1", "ada2", "ada3") if l == 0 else ()) + OWN +
         (("next0", "next1", "out0", "out1", "next2", "next3") if l < L - 1 else ("out0", "out1")) for l in range(L)]
GROUP = ("g0", "u0", "g1", "u1", "d0", "g2", "u2", "d1", "g3", "u3", "d2", "d3")
BEFORE = [sum(len(HEADS[i]) + NG * len(GROUP) for i in range(l)) for l in range(L)]
TURN = len(GROUP) // NSLOT


def place(l, name):
    c = BEFORE[l] + (HEADS[l].index(name) if name in HEADS[l] else len(HEADS[l]) + GROUP.index(name))
    return c % NSLOT, c // NSLOT


def build(nc, d, out):
    f32, i32 = mybir.dt.float32, mybir.dt.int32
    ALU, ACT, X = mybir.AluOpType, mybir.ActivationFunctionType, mybir.AxisListType.X

    ctx = ExitStack()
    with ctx:
        def sb(name, shape, dt=f32):
            return ctx.enter_context(nc.sbuf_tensor(name, shape, dt))

        def sems(names, prefix=""):
            return {n: ctx.enter_context(nc.semaphore(prefix + n)) for n in names}

        ring = [sb(f"ring{i}", [P, SLOT]) for i in range(NSLOT)]
        const = sb("const", [P, NCONST])
        param = [sb(f"param{l}", [P, NPARAM]) for l in range(L)]
        x = sb("x", [P, TT, D])
        xn = sb("xn", [P, TT, D])
        hT = sb("hT", [P, KD, S])
        yT = sb("yT", [P, KD, S])
        acc = sb("acc", [P, 3, D])
        grow = sb("grow", [P, D])
        brow = sb("brow", [1, D])
        cols = sb("cols", [P, 4, KD])
        amul = sb("amul", [P, 2, KD])
        scin = sb("scin", [P, KD])
        sc = sb("sc", [P, KD])
        stat = sb("stat", [P, 8])
        astat = sb("astat", [P, TT, 3])
        posi = sb("posi", [P, S], i32)
        cosT = sb("cosT", [P, S])
        sinT = sb("sinT", [P, S])
        raw = sb("raw", [P, 7, S])
        kcat = sb("kcat", [P, NKV, 2, S])
        vslc = sb("vslc", [P, TT, P])
        vwin = sb("vwin", [P, TT, P + 3 * NH])
        gates = sb("gates", [P, TT, NH, 3])
        hidc = sb("hidc", [P, 2, 2, NKV * NCMP])
        kcmp = sb("kcmp", [P, NKV * NCMP])
        vcmp = sb("vcmp", [NCMP, NKV, HD])
        vblk = sb("vblk", [NH * NCMP, NH, HD])
        xlp = sb("xlp", [P, 2, LRU_W - 1 + S])
        vp = sb("vp", [P, 2, CONV_K - 1 + S])
        cacc = sb("cacc", [P, 2, S])
        lamb = sb("lamb", [P, L, 6])
        ltmp = sb("ltmp", [P, L, 12])
        mx = sb("mx", [P, NH, 4])
        sums = sb("sums", [P, TT, 3, NH])
        coef = sb("coef", [P, TT, 3, NH])
        cmx = sb("cmx", [P, NH])
        we = sb("we", [P, TT, NE])
        rt = sb("rt", [P, 256])
        flag = sb("flag", [1, 2], i32)
        sel = sb("sel", [P, TT, P])
        selT = sb("selT", [P, TT, P])
        wslot = sb("wslot", [P, NE])
        gcur = sb("gcur", [P, 8])
        arena = sb("arena", [P, 3072])
        silu = [arena[:, 0:512], arena[:, 512:1024]]
        hid = [arena[:, 1024:1536], arena[:, 1536:2048]]
        hidT = [arena[:, 2048:2560], arena[:, 2560:3072]]
        ys = raw[:, 0:4, :].rearrange("p a b -> p (a b)")
        xg = yT[:, 0:4, :].rearrange("p a (b c) -> p (a b) c", c=P)
        sp = [arena[:, 512 * i:512 * (i + 1)] for i in range(3)]
        pT = [arena[:, 1536 + 512 * i:2048 + 512 * i] for i in range(3)]
        oatt = [hT[:, 2 * t:2 * t + 2, :].rearrange("p a b -> p (a b)") for t in range(TT)]
        otmp = hT[:, 6:8, :].rearrange("p a b -> p (a b)")
        scmp = hT[:, 4, 0:NH * NCMP]
        pcT = hT[:, 5, 0:P]
        xc, thr, thi, av = (xn[:, i // 2, 512 * (i % 2):512 * (i % 2) + 512].rearrange("p (a b) -> p a b", a=2)
                            for i in range(4))
        tv = yT[:, 2:4, :]
        cu, cth, csq = (arena[:, 512 * i:512 * (i + 1)].rearrange("p (a b) -> p a b", a=2) for i in range(3))
        crs, crs2 = arena[:, 1536:1792], arena[:, 1792:2048]
        vcT = arena[:, 2048:2304]
        glg = arena[:, 2304:2816].rearrange("p (a b) -> p a b", a=2)
        lrs = arena[:, 2816:3072]
        ropa, ropb = arena[:, 0:512], arena[:, 512:1024]
        blkG = arena[:, 0:2 * LP * NKV * NCMP].rearrange("p (v k h n) -> p v k h n", v=2, k=LP, h=NKV)
        bank = [ctx.enter_context(nc.psum_tensor(f"bank{i}", [P, 512], f32)) for i in range(8)]
        opsum = bank[6:8]

        q = sems(SEMS + PASS_SEMS)
        second = [sems(PASS_SEMS, f"second{l}_") for l in range(L)]
        loaded = [ctx.enter_context(nc.semaphore(f"loaded{i}")) for i in range(NSLOT)]
        loaded2 = [[ctx.enter_context(nc.semaphore(f"second{l}_loaded{i}")) for i in range(3)] for l in range(L)]

        def C(name, rows=P):
            return const[:rows, CONST[name][0]:CONST[name][1]]

        def W(l, name):
            return param[l][:, PARAM[name][0]:PARAM[name][1]]

        def abank(k):
            return bank[(k - 1) % 3]

        def dbank(k):
            return bank[3 + (k - 1) % 3]

        ident, ones = C("ident"), C("ones")
        wg_v = d["moe_w_gate"].rearrange("l g e (p k) f -> (l g e) p (k f)", k=KD)
        wu_v = d["moe_w_up"].rearrange("l g e (p k) f -> (l g e) p (k f)", k=KD)
        wd_v = d["moe_w_down"].rearrange("l g e (p k) f -> (l g e) p (k f)", k=FH // P)
        EX = {"g": wg_v, "u": wu_v, "d": wd_v}

        def k3(ap, k):
            return ap.rearrange("p (k n) -> p k n", k=k)

        def slot_of(l, name):
            return ring[place(l, name)[0]]

        block = ctx.enter_context(nc.Block())

        written, drained, used = {}, {}, {}

        def sem_at(m, mark, turn=None, back=0):
            name, value = mark
            if turn is None:
                return m[name], value
            return m[name], turn * TURNS[name] + (value - back * TURNS[name])

        @block.tensor
        def _(pe):
            n = Waits()
            mm = nc.tensor.matmul

            def proj_ch(b, l, name, c0, tiles, at=0):
                w = k3(slot_of(l, name)[:, :], KD) if name != "win" else \
                    k3(slot_of(l, name)[:, 0:KD * (C_WIN[1] - C_WIN[0])], KD)
                for i in range(tiles):
                    for k in range(KD):
                        last = mm(b[:, at + i * S:at + (i + 1) * S], w[:, k, c0 + i * P:c0 + (i + 1) * P],
                                  hT[:, k, :], start=(k == 0), stop=(k == KD - 1))
                return last

            def proj_tok(b, l, name, c0, width):
                w = k3(slot_of(l, name)[:, :], KD) if name != "win" else \
                    k3(slot_of(l, name)[:, 0:KD * (C_WIN[1] - C_WIN[0])], KD)
                for t in range(TT):
                    for k in range(KD):
                        last = mm(b[:, t * width:(t + 1) * width], hT[:, k, t * P:(t + 1) * P],
                                  w[:, k, c0:c0 + width], start=(k == 0), stop=(k == KD - 1))
                return last

            def arrived(l, name):
                s, before = place(l, name)
                pe.wait_ge(loaded[s], 16 * (before + 1))

            def act_job(*key):
                pe.wait_ge(q["act_free"], n("act_free"))
                k = n.n["act_free"]
                written[key], drained[key] = ("act_full", k), ("act_free", k + 3)
                return abank(k)

            def dve_job(*key):
                pe.wait_ge(q["dve_free"], n("dve_free"))
                k = n.n["dve_free"]
                written[key], drained[key] = ("dve_full", k), ("dve_free", k + 3)
                return dbank(k)

            def wait_drained(*key):
                pe.wait_ge(*sem_at(q, drained[key]))

            def mod_cols(l, part):
                b = dve_job("cols", l, part)
                pe.wait_ge(q["acc_ready"], n("acc_ready"))
                for k in range(KD):
                    last = mm(b[:, k:k + 1], acc[:, (6 * l + part) % 3, k:D:KD], ones[:, 0:1], start=True, stop=True)
                last.then_inc(q["dve_full"], 1)

            def mod_row(part, l):
                pe.wait_ge(q["acc_ready"], n("acc_ready"))
                pe.wait_ge(q["bias_row"], n("bias_row", 16))
                for h in range(2):
                    b = act_job("row", l, part, h)
                    last = mm(b[:, :], ones, acc[:, (6 * l + part) % 3, h * CH:(h + 1) * CH], start=True, stop=False)
                    if h:
                        last.then_inc(q["acc_read"], 1)
                    last = mm(b[:, :], C("ones", 1), brow[0:1, h * CH:(h + 1) * CH], start=False, stop=True)
                    last.then_inc(q["act_full"], 1)

            def rows_to_hT(l, norm):
                pe.wait_ge(q["xn_ready"], n("xn_ready"))
                for j in range(KD // 2):
                    b = act_job("hT", l, norm, j) if j % 2 == 0 else dve_job("hT", l, norm, j)
                    for i in range(2):
                        for t in range(TT):
                            last = nc.tensor.transpose(b[:, i * S + t * P:i * S + (t + 1) * P],
                                                       xn[:, t, 2 * j + i:D:KD], ident)
                    last.then_inc(q["act_full" if j % 2 == 0 else "dve_full"], 1)
                wait_drained("hT", l, norm, 2)
                wait_drained("hT", l, norm, 3)

            def sum_rows(b, src, last_sem):
                for ct in range(2):
                    last = mm(b[:, 0:S], ones, src[:, ct, :], start=(ct == 0), stop=(ct == 1))
                last.then_inc(q[last_sem], 1)

            def attention(l, t):
                V = (vslc, vwin)
                nb = t + 1

                def query(h):
                    o = HD * (h % 2)
                    return raw[o:o + HD, h // 2, t * P:(t + 1) * P], o, h // GQA

                for par in range(2):
                    b = dve_job("scmp", l, t, par)
                    for h in range(par, NH, 2):
                        qh, o, g = query(h)
                        last = mm(b[:, h * 16:h * 16 + NCMP], qh, kcmp[o:o + HD, g * NCMP:(g + 1) * NCMP],
                                  start=True, stop=True)
                    last.then_inc(q["dve_full"], 1)
                for i in range(NH + 3):
                    if i < NH:
                        qh, o, g = query(i)
                        b = dve_job("scores", l, t, i)
                        mm(b[:, :].rearrange("p (a b) -> p a b", a=2)[:, :, 0:nb * P], qh,
                           kcat[o:o + HD, g, :, 0:nb * P], start=True, stop=True).then_inc(q["dve_full"], 1)
                    if i == 1:
                        b = act_job("pcT", l, t)
                        pe.wait_ge(q["cmp_p"], n("cmp_p"))
                        nc.tensor.transpose(b[0:NH * NCMP, 0:P], scmp, ident).then_inc(q["act_full"], 1)
                    if 2 <= i < NH + 2:
                        h = i - 2
                        key = ("pT", (l * TT + t) * NH + h)
                        b = act_job(*key) if h % 2 == 0 else dve_job(*key)
                        pe.wait_ge(q["p_ready"], n("p_ready"))
                        for ty in range(2):
                            for kb in range(nb):
                                last = nc.tensor.transpose(b[:, (ty * nb + kb) * P:(ty * nb + kb + 1) * P],
                                                           sp[h % 3][:, ty * S + kb * P:ty * S + (kb + 1) * P], ident)
                        last.then_inc(q["act_full" if h % 2 == 0 else "dve_full"], 1)
                    if i >= 3:
                        h = i - 3
                        if h == 0 and (l or t):
                            pe.wait_ge(q["o_free"], n("o_free"))
                        wait_drained("pT", (l * TT + t) * NH + h)
                        for ty in range(2):
                            for kb in range(nb):
                                last = mm(opsum[ty][:, h * HD:(h + 1) * HD],
                                          pT[h % 3][:, (ty * nb + kb) * P:(ty * nb + kb + 1) * P],
                                          V[ty][:, kb, (h // GQA) * HD:(h // GQA + 1) * HD],
                                          start=(kb == 0), stop=(kb == nb - 1))
                        last.then_inc(q["pT_read"], 1)
                b = dve_job("ocmp", l, t)
                wait_drained("pcT", l, t)
                mm(b[:, :], pcT[0:NH * NCMP, :], vblk[:, :, :].rearrange("p a b -> p (a b)"),
                   start=True, stop=True).then_inc(q["dve_full"], 1)

            def moe_pass(m, n, l, kind, wait_chunk):
                def act_job(*key):
                    pe.wait_ge(m["act_free"], n("act_free"))
                    k = n.n["act_free"]
                    key = (kind, l) + key
                    written[key], drained[key] = ("act_full", k), ("act_free", k + 3)
                    return abank(k)

                def dve_job(*key):
                    pe.wait_ge(m["dve_free"], n("dve_free"))
                    k = n.n["dve_free"]
                    key = (kind, l) + key
                    written[key], drained[key] = ("dve_full", k), ("dve_free", k + 3)
                    return dbank(k)

                def wait_drained(*key):
                    pe.wait_ge(*sem_at(m, drained[(kind, l) + key], n.turn))

                pe.wait_ge(m["sel_ready"], n("sel_ready"))
                b = dve_job("weights")
                for t in range(TT):
                    last = mm(b[:, 0:NE], sel[:, t, :], we[:, t, :], start=(t == 0), stop=(t == TT - 1))
                last.then_inc(m["dve_full"], 1)
                b = dve_job("selT")
                for t in range(TT):
                    last = nc.tensor.transpose(b[:, t * P:(t + 1) * P], sel[:, t, :], ident)
                last.then_inc(m["dve_full"], 1)
                for ks in ((0, 1, 2, 3), (4, 5), (6, 7)):
                    b = act_job("gather", 0) if ks[0] == 0 else dve_job("gather", ks[0])
                    for i, k in enumerate(ks):
                        for t in range(TT):
                            last = mm(b[:, i * P:(i + 1) * P], xn[:, t, k:D:KD], sel[:, t, :],
                                      start=(t == 0), stop=(t == TT - 1))
                    last.then_inc(m["act_full" if ks[0] == 0 else "dve_full"], 1)
                wait_drained("gather", 0)
                wait_drained("gather", 6)

                def up(e):
                    for c in "gu":
                        b = act_job("g", e) if c == "g" else dve_job("u", e)
                        wait_chunk(c + str(e))
                        w = k3(slot_of(l, c + str(e))[:, :], KD)
                        for k in range(KD):
                            last = mm(b[:, :], xg[:, k, :], w[:, k, :], start=(k == 0), stop=(k == KD - 1))
                        last.then_inc(m["act_full" if c == "g" else "dve_full"], 1)
                        used[kind, l, c + str(e)] = written[kind, l, c, e]

                def down(e):
                    b = act_job("hidT", e)
                    wait_drained("u", e)
                    for j in range(FH // P):
                        last = nc.tensor.transpose(b[:, j * P:(j + 1) * P], hid[e % 2][:, j:FH:FH // P], ident)
                    last.then_inc(m["act_full"], 1)
                    wait_drained("hidT", e)
                    wait_chunk("d" + str(e))
                    w = k3(slot_of(l, "d" + str(e))[:, :], FH // P)
                    for h in range(2):
                        for j in range(FH // P):
                            last = mm(opsum[h][:, :], hidT[e % 2][:, j * P:(j + 1) * P], w[:, j, h * CH:(h + 1) * CH],
                                      start=(e == 0 and j == 0), stop=(e == NE - 1 and j == FH // P - 1))
                    last.then_inc(m["hidT_read"], 1)
                    hidT_reads[0] += 1
                    used[kind, l, "d" + str(e)] = ("hidT_read", hidT_reads[0])

                hidT_reads = [n.n.get("hidT_read", 0)]
                up(0)
                up(1)
                down(0)
                up(2)
                down(1)
                up(3)
                down(2)
                down(3)
                n.n["hidT_read"] = hidT_reads[0]
                pe.wait_ge(m["ys_ready"], n("ys_ready"))
                for t in range(TT):
                    for h in range(2):
                        b = dve_job("scatter", t, h)
                        mm(b[:, :], selT[:, t, :], ys[:, h * CH:(h + 1) * CH], start=True, stop=True)\
                            .then_inc(m["dve_full"], 1)

            pe.wait_ge(q["consts"], 16 * (1 + L))
            mod_cols(0, 0)
            mod_cols(0, 1)
            for l in range(L):
                rows_to_hT(l, 0)
                arrived(l, "conv")
                for h in range(2):
                    last = proj_ch(act_job("conv", l, h), l, "conv", h * D_CONV, 2).then_inc(q["act_full"], 1)
                used["head", l, "conv"] = written["conv", l, 1]
                arrived(l, "lru")
                for h in range(2):
                    last = proj_ch(act_job("lru", l, h), l, "lru", h * D_LRU, 2).then_inc(q["act_full"], 1)
                used["head", l, "lru"] = written["lru", l, 1]
                arrived(l, "q")
                for h in range(2):
                    last = proj_ch(act_job("q", l, h), l, "q", h * 2 * P, 2).then_inc(q["act_full"], 1)
                used["head", l, "q"] = written["q", l, 1]
                arrived(l, "kv")
                b = act_job("kcks", l)
                proj_ch(b, l, "kv", 0, 1)
                proj_ch(b, l, "kv", 2 * P, 1, at=S).then_inc(q["act_full"], 1)
                proj_ch(act_job("vc", l), l, "kv", P, 1).then_inc(q["act_full"], 1)
                proj_tok(act_job("vs", l), l, "kv", 3 * P, P).then_inc(q["act_full"], 1)
                used["head", l, "kv"] = written["vs", l]
                pe.wait_ge(q["lru_conv"], n("lru_conv"))
                for name in ("wa", "wx"):
                    b = act_job(name, l)
                    w = W(l, name).rearrange("p (a b) -> p a b", a=2)
                    for ct in range(2):
                        last = mm(b[:, ct * S:(ct + 1) * S], w[:, ct, :], xc[:, ct, :], start=True, stop=True)
                    last.then_inc(q["act_full"], 1)
                b = dve_job("conv_mean", l)
                pe.wait_ge(q["conv_sum"], n("conv_sum"))
                sum_rows(b, cacc, "dve_full")
                arrived(l, "win")
                proj_ch(act_job("kw", l), l, "win", 0, 1).then_inc(q["act_full"], 1)
                proj_tok(act_job("vwin", l), l, "win", P, P + 3 * NH).then_inc(q["act_full"], 1)
                used["head", l, "win"] = written["vwin", l]
                wait_drained("kw", l)
                for lo, hi in ((0, 2), (2, 4), (4, 6), (6, 7)):
                    b = dve_job("rope", l, lo)
                    mm(b[:, 0:(hi - lo) * S], C("rot"), raw[:, lo:hi, :], start=True, stop=True)\
                        .then_inc(q["dve_full"], 1)
                b = act_job("conv_sd", l)
                pe.wait_ge(q["conv_sq"], n("conv_sq"))
                sum_rows(b, csq, "act_full")
                b = act_job("lru_rms", l)
                pe.wait_ge(q["lru_sq"], n("lru_sq"))
                sum_rows(b, thr, "act_full")
                pe.wait_ge(q["rope_ready"], n("rope_ready"))
                dup = C("dup").rearrange("p (a b) -> p a b", a=2)
                for h in range(NKV):
                    b = act_job("kcat", l, h)
                    mm(b[:, :], dup[:, h, :], raw[:, 5:7, :], start=True, stop=True).then_inc(q["act_full"], 1)
                for h in range(NKV):
                    b = dve_job("blk", l, h)
                    mm(b[:, 0:S], dup[:, h, :], raw[:, 4, :], start=True, stop=True)
                    mm(b[:, S:2 * S], dup[:, h, :], vcT, start=True, stop=True).then_inc(q["dve_full"], 1)
                b = act_job("conv_rms", l)
                pe.wait_ge(q["conv_sq2"], n("conv_sq2"))
                sum_rows(b, csq, "act_full")
                wait_drained("blk", l, 1)
                for kv, name in enumerate(("cmpk", "cmpv")):
                    b = act_job(name, l)
                    arrived(l, name)
                    w = k3(slot_of(l, name)[:, :], LP)
                    for m_ in range(2):
                        for k in range(LP):
                            last = mm(b[:, m_ * 32:m_ * 32 + NKV * NCMP], w[:, k, m_ * P:(m_ + 1) * P],
                                      blkG[:, kv, k, :, :].rearrange("p a b -> p (a b)"),
                                      start=(k == 0), stop=(k == LP - 1))
                    last.then_inc(q["act_full"], 1)
                    used["head", l, name] = written[name, l]
                wait_drained("cmpv", l)
                b = act_job("kcmp", l)
                w2 = W(l, "w2k").rearrange("p (a b) -> p a b", a=2)
                for m_ in range(2):
                    last = mm(b[:, 0:NKV * NCMP], w2[:, m_, :], hidc[:, 0, m_, :], start=(m_ == 0), stop=(m_ == 1))
                last.then_inc(q["act_full"], 1)
                b = dve_job("vcmp", l)
                w2 = W(l, "w2v").rearrange("p (a b) -> p a b", a=2)
                for h in range(NKV):
                    for m_ in range(2):
                        last = mm(b[0:NCMP, h * HD:(h + 1) * HD], hidc[:, 1, m_, h * NCMP:(h + 1) * NCMP],
                                  w2[:, m_, :], start=(m_ == 0), stop=(m_ == 1))
                last.then_inc(q["dve_full"], 1)
                b = dve_job("vblk", l)
                wait_drained("vcmp", l)
                rep = C("rep", NCMP).rearrange("p (a b) -> p a b", a=2)
                for h in range(NKV):
                    last = mm(b[0:NH * NCMP, 0:HD], rep[:, h, :], vcmp[:, h, :], start=(h == 0), stop=(h == NKV - 1))
                last.then_inc(q["dve_full"], 1)
                mod_row(2, l)
                mod_cols(l, 3)
                wait_drained("kcmp", l)
                wait_drained("kcat", l, 1)
                wait_drained("vblk", l)
                for t in range(TT):
                    attention(l, t)
                for t in range(TT):
                    b = dve_job("attT", l, t)
                    pe.wait_ge(q["att_n"], n("att_n"))
                    for j in range(D_ATT // P):
                        last = nc.tensor.transpose(b[:, j * P:(j + 1) * P], oatt[t][:, j * P:(j + 1) * P], ident)
                    last.then_inc(q["dve_full"], 1)
                mod_cols(l, 4)
                pe.wait_ge(q["y_ready"], n("y_ready", 2))
                wait_drained("attT", l, 1)
                for h in range(2):
                    name = "out" + str(h)
                    arrived(l, name)
                    w = k3(slot_of(l, name)[:, :], KD)
                    for t in range(TT):
                        b = dve_job("out", l, h, t)
                        for k in range(KD):
                            last = mm(b[:, :], yT[:, k, t * P:(t + 1) * P], w[:, k, :],
                                      start=(k == 0), stop=(k == KD - 1))
                        last.then_inc(q["dve_full"], 1)
                    used["head", l, name] = written["out", l, h, TT - 1]
                rows_to_hT(l, 1)
                mod_row(5, l)
                if l < L - 1:
                    mod_cols(l + 1, 0)
                    mod_cols(l + 1, 1)
                b = dve_job("logits", l)
                w = W(l, "rw").rearrange("p (k n) -> p k n", k=KD)
                for t in range(TT):
                    for k in range(KD):
                        last = mm(b[:, t * NR:(t + 1) * NR], hT[:, k, t * P:(t + 1) * P], w[:, k, :],
                                  start=(k == 0), stop=(k == KD - 1))
                last.then_inc(q["dve_full"], 1)
                b = dve_job("ranks", l)
                pe.wait_ge(q["lg_ready"], n("lg_ready"))
                oh = rt[:, 0:TT * NG].rearrange("p (t g) -> p t g", t=TT)
                mm(b[:, 0:NG], C("tri"), oh[:, 0, :], start=True, stop=True)
                mm(b[:, NG:2 * NG], ones, oh[:, 0, :], start=True, stop=False)
                mm(b[:, NG:2 * NG], C("tri"), oh[:, 1, :], start=False, stop=True)
                mm(b[:, 2 * NG:3 * NG], ones, oh[:, 0, :], start=True, stop=False)
                mm(b[:, 2 * NG:3 * NG], ones, oh[:, 1, :], start=False, stop=True).then_inc(q["dve_full"], 1)

                def wait_chunk(name):
                    s, before = place(l, name)
                    pe.wait_ge(loaded[s], n.turn * (16 * TURN) + 16 * (before + 1))

                with pe.Fori(0, NG) as g:
                    n.loop(g, TURNS)
                    moe_pass(q, n, l, "loop", wait_chunk)
                    n.end(NG)
                n("sel_ready")
                pe.wait_ge(q["routed"], l + 1)
                full = pe.value_load(flag[0:1, 0:1], min_val=0, max_val=1)
                with pe.If(full > 0):
                    def wait_chunk2(name):
                        j = GROUP.index(name)
                        pe.wait_ge(loaded2[l][j % 3], 16 * (j // 3 + 1))

                    moe_pass(second[l], Waits(), l, "second", wait_chunk2)

        @block.scalar
        def _(act):
            n = Waits()
            A = nc.scalar.activation

            def step(ins):
                return ins.then_inc(q["act_steps"], 1)

            def own():
                act.wait_ge(q["act_steps"], n("act_steps"))

            def full():
                act.wait_ge(q["act_full"], n("act_full"))
                return abank(n.n["act_full"])

            def own_drain():
                act.wait_ge(q["act_free"], n.n["act_full"] + 3)

            def evac(dst, src_cols=512, rows=P):
                b = full()
                return A(dst, b[0:rows, 0:src_cols], ACT.Copy).then_inc(q["act_free"], 1)

            def row_roots():
                for t in range(TT):
                    last = A(arena[:, t * D:(t + 1) * D], x[:, t, :], ACT.Square, accum_out=stat[:, t:t + 1])
                step(last)
                own()
                A(stat[:, 2:4], stat[:, 0:2], ACT.Sqrt, bias=C("eps"), scale=1.0 / D).then_inc(q["norm_root"], 1)

            def rows_to_hT(norm):
                act.wait_ge(q["modcols"], n("modcols"))
                for j in (0, 2):
                    b = full()
                    for i in range(2):
                        k = 2 * j + i
                        last = A(hT[:, k, :], b[:, i * S:(i + 1) * S], ACT.Identity,
                                 bias=cols[:, 2 * norm, k:k + 1], scale=amul[:, norm, k:k + 1])
                    last.then_inc(q["act_free"], 1)

            def moe_pass(m, n, l, kind):
                def full():
                    act.wait_ge(m["act_full"], n("act_full"))
                    return abank(n.n["act_full"])

                b = full()
                for k in range(4):
                    last = A(xg[:, k, :], b[:, k * P:(k + 1) * P], ACT.Identity,
                             bias=cols[:, 2, k:k + 1], scale=amul[:, 1, k:k + 1])
                last.then_inc(m["act_free"], 1)

                def gate(e):
                    if e >= 2 or kind == "loop":
                        act.wait_ge(*sem_at(m, drained[kind, l, "u", (e - 2) % NE], n.turn, int(e < 2)))
                    b = full()
                    A(silu[e % 2], b[:, :], ACT.Silu).then_inc(m["act_free"], 1)

                def hidden(e):
                    b = full()
                    A(hidT[e % 2], b[:, :], ACT.Copy).then_inc(m["act_free"], 1)

                gate(0)
                gate(1)
                hidden(0)
                gate(2)
                hidden(1)
                gate(3)
                hidden(2)
                hidden(3)

            def credits(m):
                act.sem_inc(m["act_free"], 3)

            credits(q)
            act.wait_ge(q["c_in"], 16)
            A(sc[:, :], scin[:, :], ACT.Silu).then_inc(q["sc_ready"], 1)
            act.wait_ge(q["angle"], n("angle"))
            A(sinT[:, :], arena[:, 0:S], ACT.Sin)
            A(cosT[:, :], arena[:, S:2 * S], ACT.Sin).then_inc(q["trig"], 1)
            act.wait_ge(q["lam_a"], n("lam_a"))
            A(ltmp[:, :, 2:4], ltmp[:, :, 0:2], ACT.Exp, scale=-1.0).then_inc(q["lam_e"], 1)
            act.wait_ge(q["lam_w"], n("lam_w"))
            A(ltmp[:, :, 8:10], ltmp[:, :, 4:6], ACT.Ln).then_inc(q["lam_ln"], 1)
            act.wait_ge(q["consts"], 16 * (1 + L))

            for l in range(L):
                if l:
                    act.wait_ge(q["x_done"], n("x_done"))
                act.dma_start(brow[:, :], d["ada_b"][l:l + 1, 2 * D:3 * D]).then_inc(q["bias_row"], 16)
                row_roots()
                rows_to_hT(0)
                evac(cu)
                b = full()
                A(cth, b[:, :], ACT.Tanh, scale=0.5).then_inc(q["act_free"], 1)
                evac(xlp[:, :, LRU_W - 1:])
                b = full()
                A(glg, b[:, :], ACT.Gelu_apprx_tanh).then_inc(q["act_free"], 1)
                evac(raw[:, 0:2, :])
                evac(raw[:, 2:4, :])
                evac(raw[:, 4:6, :])
                evac(vcT, S)
                evac(vslc[:, :, :], TT * P)
                for i, dst in enumerate((thr, thi)):
                    b = full()
                    for ct in range(2):
                        last = A(dst[:, ct, :], b[:, ct * S:(ct + 1) * S], ACT.Tanh,
                                 bias=lamb[:, l, 2 + 2 * i + ct:3 + 2 * i + ct], scale=0.5)
                    last.then_inc(q["act_free"], 1)
                own_drain()
                for ct in range(2):
                    A(av[:, ct, :], thr[:, ct, :], ACT.Exp, bias=lamb[:, l, ct:ct + 1], scale=lamb[:, l, ct:ct + 1])
                for ct in range(2):
                    last = A(tv[:, ct, :], thr[:, ct, :], ACT.Tanh, bias=lamb[:, l, ct:ct + 1],
                             scale=lamb[:, l, ct:ct + 1])
                last.then_inc(q["lru_at"], 1)
                evac(raw[:, 6, :], S)
                evac(vwin[:, :, :], TT * (P + 3 * NH))
                own_drain()
                A(gates[:, :, :, :].rearrange("p t h j -> p t (h j)"), vwin[:, :, P:], ACT.Tanh, scale=0.5)\
                    .then_inc(q["gate_th"], 1)
                act.wait_ge(q["lru_q"], n("lru_q"))
                A(thr, thr, ACT.Sqrt, scale=-1.0).then_inc(q["lru_root"], 1)
                b = full()
                A(crs, b[:, 0:S], ACT.Sqrt, bias=C("eps"), scale=1.0 / D_CONV).then_inc(q["act_free"], 1)
                b = full()
                A(lrs, b[:, 0:S], ACT.Sqrt, bias=C("eps"), scale=1.0 / D_LRU).then_inc(q["act_free"], 1)
                evac(kcat[:, 0, :, :])
                evac(kcat[:, 1, :, :])
                act.wait_ge(q["conv_ln"], n("conv_ln"))
                for ct in range(2):
                    last = A(cacc[:, ct, :], cacc[:, ct, :], ACT.Silu, bias=W(l, "lnb")[:, ct:ct + 1],
                             scale=W(l, "lng")[:, ct:ct + 1])
                last.then_inc(q["conv_silu"], 1)
                b = full()
                A(crs2, b[:, 0:S], ACT.Sqrt, bias=C("eps"), scale=1.0 / D_CONV).then_inc(q["act_free"], 1)
                for kv in range(2):
                    b = full()
                    A(hidc[:, kv, :, :], b[:, 0:64].rearrange("p (a b) -> p a b", a=2)[:, :, 0:NKV * NCMP],
                      ACT.Gelu_apprx_tanh).then_inc(q["act_free"], 1)
                evac(kcmp[:, :], NKV * NCMP)
                evac(grow[:, 0:CH])
                evac(grow[:, CH:D])

                for t in range(TT):
                    w = (t + 1) * P
                    act.wait_ge(q["cmp_s"], n("cmp_s"))
                    A(scmp, scmp, ACT.Exp, scale=HD ** -0.5).then_inc(q["cmp_p"], 1)
                    for i in range(NH + 2):
                        if i < NH:
                            act.wait_ge(q["s_ready"], n("s_ready"))
                            for ty in range(2):
                                seg = sp[i % 3][:, ty * S:ty * S + w]
                                last = A(seg, seg, ACT.Exp, bias=mx[:, i, 2 + ty:3 + ty],
                                         accum_out=sums[:, t, 1 + ty, i:i + 1])
                            last.then_inc(q["p_ready"], 1)
                        if i == 1:
                            evac(pcT[0:NH * NCMP, :], P, NH * NCMP)
                        if i >= 2 and i % 2 == 0:
                            h = (l * TT + t) * NH + i - 2
                            if h >= 3:
                                act.wait_ge(q["pT_read"], h - 2)
                            evac(pT[(i - 2) % 3][:, 0:2 * w], 2 * w)
                for t in range(TT):
                    act.wait_ge(q["att_ss"], n("att_ss"))
                    A(astat[:, t, 1:2], astat[:, t, 0:1], ACT.Sqrt, bias=C("eps"), scale=1.0 / D_ATT)\
                        .then_inc(q["att_root"], 1)
                act.dma_start(brow[:, :], d["ada_b"][l:l + 1, 5 * D:6 * D]).then_inc(q["bias_row"], 16)
                act.wait_ge(q["x_done"], n("x_done"))
                row_roots()
                rows_to_hT(1)
                evac(grow[:, 0:CH])
                evac(grow[:, CH:D])
                act.wait_ge(q["lg_ready"], n("lg_ready"))
                A(rt[:, 60:68], rt[:, 50:58], ACT.Exp).then_inc(q["lg_exp"], 1)
                act.wait_ge(q["top_d"], n("top_d"))
                A(rt[:, 142:144], rt[:, 140:142], ACT.Exp).then_inc(q["top_exp"], 1)

                with act.Fori(0, NG) as g:
                    n.loop(g, TURNS)
                    moe_pass(q, n, l, "loop")
                    n.end(NG)
                act.wait_ge(q["routed"], l + 1)
                more = act.value_load(flag[0:1, 0:1], min_val=0, max_val=1)
                with act.If(more > 0):
                    credits(second[l])
                    moe_pass(second[l], Waits(), l, "second")

            act.wait_ge(*sem_at(q, written["cols", L - 1, 4]))
            act.dma_start(acc[:, 1, :], d["final_norm_g"]).then_inc(q["gain_in"], 16)
            act.wait_ge(q["x_done"], n("x_done"))
            row_roots()

        @block.vector
        def _(vec):
            n = Waits()
            made = Waits()
            V = nc.vector

            def step(ins, name="dve_steps"):
                made(name)
                return ins.then_inc(q[name], 1)

            def own(name="dve_steps"):
                vec.wait_ge(q[name], made.now(name))

            def do(ins, name="dve_steps"):
                step(ins, name)
                own(name)

            def wait_drained(*key):
                vec.wait_ge(*sem_at(q, drained[key]))

            def full():
                vec.wait_ge(q["dve_full"], n("dve_full"))
                return dbank(n.n["dve_full"])

            def wait(name):
                vec.wait_ge(q[name], n(name))

            def ts(out_, in_, s1, s2, op0, op1=ALU.bypass):
                return V.tensor_scalar(out_, in_, s1, s2, op0, op1)

            def halves(ap):
                return ap.rearrange("p (a b) -> p a b", a=2)

            def modulation(part):
                for h in range(2):
                    name = "ada" + str(2 * part + h)
                    s, before = place(0, name)
                    vec.wait_ge(loaded[s], 16 * (before + 1))
                    w = k3(ring[s][:, :], KD)
                    dst = acc[:, part, h * CH:(h + 1) * CH]
                    do(ts(dst, w[:, 0, :], sc[:, 0:1], None, ALU.mult))
                    for k in range(1, KD):
                        sig = "acc_ready" if h and k == KD - 1 else "dve_steps"
                        do(V.scalar_tensor_tensor(dst, w[:, k, :], sc[:, k:k + 1], dst, ALU.mult, ALU.add), sig)
                    used["head", 0, name] = (sig, made.n[sig])

            def mod_cols(l, col):
                b = full()
                do(V.tensor_tensor(cols[:, col, :], b[:, 0:KD], W(l, "adab")[:, col * KD:(col + 1) * KD], ALU.add), "dve_free")

            def gain_cols(l, norm, name):
                do(V.scalar_tensor_tensor(amul[:, norm, :], cols[:, 2 * norm + 1, :], 1.0, W(l, name),
                                          ALU.add, ALU.mult), "modcols")

            def normalize_rows():
                wait("norm_root")
                do(V.reciprocal(stat[:, 4:6], stat[:, 2:4]))
                for t in range(TT):
                    do(ts(xn[:, t, :], x[:, t, :], stat[:, 4 + t:5 + t], None, ALU.mult),
                       "xn_ready" if t == TT - 1 else "dve_steps")

            def rows_to_hT(norm):
                for j in (1, 3):
                    b = full()
                    for i in range(2):
                        k = 2 * j + i
                        step(ts(hT[:, k, :], b[:, i * S:(i + 1) * S], amul[:, norm, k:k + 1],
                                cols[:, 2 * norm, k:k + 1], ALU.mult, ALU.add), "dve_free" if i else "dve_steps")

            def attention(l, t):
                nb = t + 1
                w = nb * P
                sc3 = scmp.rearrange("p (h n) -> p h n", h=NH)
                mask = C("cmask")[:, t * NCMP:(t + 1) * NCMP]
                for par in range(2):
                    b = full()
                    do(V.tensor_tensor(sc3[:, par::2, :],
                                       b[:, 0:NH * 16].rearrange("p (h n) -> p h n", h=NH)[:, par::2, 0:NCMP],
                                       mask.unsqueeze(1).to_broadcast([P, NH // 2, NCMP]), ALU.add), "dve_free")
                do(V.tensor_reduce(cmx[:, :], sc3, X, ALU.max))
                do(V.tensor_tensor(sc3, sc3, cmx[:, :].unsqueeze(2).to_broadcast([P, NH, NCMP]), ALU.subtract), "cmp_s")
                for i in range(NH + 2):
                    if i < NH:
                        h = (l * TT + t) * NH + i
                        b = full()
                        if h >= 3:
                            vec.wait_ge(*sem_at(q, written["pT", h - 3]))
                        for ty in range(2):
                            step(V.tensor_tensor_reduce(out=sp[i % 3][:, ty * S:ty * S + w],
                                                         in0=b[:, ty * S:ty * S + w],
                                                         in1=C("causal")[:, 2 * P - w:2 * P], scale=HD ** -0.5,
                                                         scalar=-3e38, op0=ALU.add, op1=ALU.max,
                                                         accum_out=mx[:, i, ty:ty + 1]),
                                 "dve_free" if ty else "dve_steps")
                        own("dve_free")
                        do(ts(mx[:, i, 2:4], mx[:, i, 0:2], -1.0, None, ALU.mult), "s_ready")
                    if i == 3:
                        vec.wait_ge(q["cmp_p"], l * TT + t + 1)
                        do(V.tensor_reduce(sums[:, t, 0, :], sc3, X, ALU.add))
                    if i >= 2 and i % 2 == 1:
                        h = (l * TT + t) * NH + i - 2
                        b = full()
                        if h >= 3:
                            vec.wait_ge(q["pT_read"], h - 2)
                        do(V.tensor_copy(pT[(i - 2) % 3][:, 0:2 * w], b[:, 0:2 * w]), "dve_free")
                vec.wait_ge(q["pT_read"], (l * TT + t + 1) * NH)
                cf = coef[:, t, :, :]
                do(V.reciprocal(cf, sums[:, t, :, :]))
                do(V.tensor_tensor(cf, cf, gates[:, t, :, :].rearrange("p h j -> p j h"), ALU.mult))
                do(ts(coef[:, t, 0, :], coef[:, t, 0, :], C("anyv")[:, t:t + 1], None, ALU.mult))

                def heads(ap):
                    return ap.rearrange("p (h e) -> p h e", h=NH)

                def weight(j):
                    return coef[:, t, j, :].unsqueeze(2).to_broadcast([P, NH, HD])

                b = full()
                do(V.tensor_tensor(heads(oatt[t]), heads(b[:, :]), weight(0), ALU.mult), "dve_free")
                for j in range(2):
                    do(V.tensor_tensor(heads(otmp), heads(opsum[j][:, :]), weight(1 + j), ALU.mult),
                       "o_free" if j else "dve_steps")
                    do(V.tensor_tensor(oatt[t], oatt[t], otmp, ALU.add))
                do(V.tensor_tensor_reduce(out=otmp, in0=oatt[t], in1=oatt[t], scale=1.0, scalar=0.0, op0=ALU.mult,
                                          op1=ALU.add, accum_out=astat[:, t, 0:1]), "att_ss")

            gsel, own1 = rt[:, 58:60], rt[:, 158:160]

            def select_tokens():
                do(ts(gcur[:, 1:3], gsel, gcur[:, 0:1], None, ALU.is_equal))
                do(V.tensor_tensor(gcur[:, 3:5], gcur[:, 1:3], own1, ALU.mult))
                for t in range(TT):
                    do(ts(sel[:, t, :], C("iota"), gcur[:, 3 + t:4 + t], None, ALU.is_equal),
                       "sel_ready" if t == TT - 1 else "dve_steps")

            def moe_pass(m, n, made, l, kind):
                def step(ins, name="dve_steps"):
                    made(name)
                    return ins.then_inc(m[name], 1)

                def do(ins, name="dve_steps"):
                    step(ins, name)
                    vec.wait_ge(m[name], made.now(name))

                def full():
                    vec.wait_ge(m["dve_full"], n("dve_full"))
                    return dbank(n.n["dve_full"])

                b = full()
                step(V.tensor_copy(wslot[:, :], b[:, 0:NE]), "dve_free")
                b = full()
                step(V.tensor_copy(selT[:, :, :], b[:, 0:TT * P].rearrange("p (a b) -> p a b", a=2)), "dve_free")
                for k0 in (4, 6):
                    b = full()
                    for i in range(2):
                        k = k0 + i
                        ins = ts(xg[:, k, :], b[:, i * P:(i + 1) * P], amul[:, 1, k:k + 1],
                                 cols[:, 2, k:k + 1], ALU.mult, ALU.add)
                        step(ins, "dve_free" if i else "dve_steps")
                vec.wait_ge(m["dve_free"], made.now("dve_free"))
                for e in range(NE):
                    vec.wait_ge(*sem_at(m, drained[kind, l, "g", e], n.turn))
                    b = full()
                    if e >= 2 or kind == "loop":
                        vec.wait_ge(*sem_at(m, written[kind, l, "hidT", (e - 2) % NE], n.turn, int(e < 2)))
                    step(V.scalar_tensor_tensor(hid[e % 2], b[:, :], wslot[:, e:e + 1], silu[e % 2],
                                                ALU.mult, ALU.mult), "dve_free")
                    if e == 1 and kind == "loop":
                        do(ts(gcur[:, 0:1], gcur[:, 0:1], 1.0, None, ALU.add))
                        do(ts(gcur[:, 1:3], gsel, gcur[:, 0:1], None, ALU.is_equal))
                        do(V.tensor_tensor(gcur[:, 3:5], gcur[:, 1:3], own1, ALU.mult))
                        for t in range(TT):
                            step(ts(sel[:, t, :], C("iota"), gcur[:, 3 + t:4 + t], None, ALU.is_equal),
                                 "sel_ready" if t == TT - 1 else "dve_steps")
                vec.wait_ge(*sem_at(m, used[kind, l, "d" + str(NE - 1)], n.turn))
                for h in range(2):
                    step(V.tensor_tensor(ys[:, h * CH:(h + 1) * CH], opsum[h][:, :],
                                         grow[:, h * CH:(h + 1) * CH], ALU.mult), "ys_ready" if h else "dve_steps")
                for t in range(TT):
                    for h in range(2):
                        b = full()
                        dst = x[:, t, h * CH:(h + 1) * CH]
                        step(V.tensor_tensor(dst, b[:, :], dst, ALU.add), "dve_free")
                vec.wait_ge(m["dve_free"], made.now("dve_free"))

            def credits(m):
                vec.sem_inc(m["dve_free"], 3)

            credits(q)
            made("dve_free", 3)
            step(V.memset(xlp[:, :, 0:LRU_W - 1], 0.0))
            step(V.memset(vp[:, :, 0:CONV_K - 1], 0.0))
            wait("sc_ready")
            modulation(0)
            vec.wait_ge(q["x_in"], 32)
            vec.wait_ge(q["consts"], 16 * (1 + L))
            MAGIC, PI = 1.5 * 2.0 ** 23, 3.1415925
            C1 = 6.28125
            C2 = float(np.float32(np.float64(2 * np.pi) - C1).view(np.uint32).__and__(0xFFFFF000).astype(np.uint32)
                       .view(np.float32))
            C3 = float(2 * np.pi - C1 - C2)
            ang, rnd, r2 = arena[:, 0:S], arena[:, 2 * S:3 * S], arena[:, S:2 * S]
            do(V.tensor_copy(r2, posi[:, :]))
            do(ts(ang, r2, C("inv"), None, ALU.mult))
            do(ts(rnd, ang, 1.0 / (2 * np.pi), MAGIC, ALU.mult, ALU.add))
            do(ts(rnd, rnd, MAGIC, None, ALU.subtract))
            for part in (C1, C2, C3):
                do(V.scalar_tensor_tensor(ang, rnd, -part, ang, ALU.mult, ALU.add))
            do(ts(ang, ang, PI, -PI, ALU.min, ALU.max))
            do(ts(r2, ang, np.pi / 2, None, ALU.add))
            do(ts(rnd, r2, PI, -2 * np.pi, ALU.is_gt, ALU.mult))
            do(V.tensor_tensor(r2, r2, rnd, ALU.add))
            do(ts(r2, r2, PI, -PI, ALU.min, ALU.max), "angle")
            for l in range(L):
                do(V.scalar_tensor_tensor(ltmp[:, l, 0:2], W(l, "lam"), -1.0, W(l, "lam"), ALU.mult, ALU.max), "lam_a" if l == L - 1 else "dve_steps")
            wait("lam_e")
            le, lw_, ld, ll, lz = (ltmp[:, :, i:i + 2] for i in (2, 4, 6, 8, 10))
            do(ts(lw_, le, 1.0, None, ALU.add))
            do(ts(ld, lw_, 1.0, None, ALU.subtract), "lam_w")
            do(ts(lz, ld, 0.0, None, ALU.is_equal))
            wait("lam_ln")
            do(V.tensor_tensor(ll, ll, lz, ALU.add))
            do(V.tensor_tensor(ld, ld, lz, ALU.add))
            do(V.reciprocal(ld, ld))
            do(V.tensor_tensor(ll, ll, ld, ALU.mult))
            do(V.tensor_tensor(ll, ll, le, ALU.mult))
            for l in range(L):
                do(ts(ltmp[:, l, 4:6], W(l, "lam"), -1.0, 0.0, ALU.mult, ALU.max))
                do(V.tensor_tensor(ltmp[:, l, 4:6], ltmp[:, l, 4:6], ltmp[:, l, 8:10], ALU.add))
                do(ts(lamb[:, l, 0:2], ltmp[:, l, 4:6], -4.0, None, ALU.mult))
                do(ts(lamb[:, l, 2:4], W(l, "ba"), 0.5, None, ALU.mult))
                do(ts(lamb[:, l, 4:6], W(l, "bx"), 0.5, None, ALU.mult))
            normalize_rows()
            modulation(1)
            mod_cols(0, 0)
            mod_cols(0, 1)
            gain_cols(0, 0, "n1g")

            for l in range(L):
                if l:
                    normalize_rows()
                rows_to_hT(0)
                wait_drained("conv", l, 1)
                do(ts(csq, cth, 0.5, 0.5, ALU.mult, ALU.add))
                do(V.tensor_tensor(vp[:, :, CONV_K - 1:], cu, csq, ALU.mult))
                cw = W(l, "ccw").rearrange("p (a b) -> p a b", a=2)
                for j in range(CONV_K):
                    for ct in range(2):
                        if j:
                            vec.wait_ge(q["dve_steps"], made.now("dve_steps") - 1 + (j == CONV_K - 1 and ct))
                            step(V.scalar_tensor_tensor(cacc[:, ct, :], vp[:, ct, j:j + S], cw[:, ct, j:j + 1],
                                                        cacc[:, ct, :], ALU.mult, ALU.add),
                                 "conv_sum" if j == CONV_K - 1 and ct else "dve_steps")
                        else:
                            step(ts(cacc[:, ct, :], vp[:, ct, 0:S], cw[:, ct, 0:1], W(l, "ccb")[:, ct:ct + 1],
                                    ALU.mult, ALU.add))
                own("conv_sum")
                wait_drained("lru", l, 0)
                lw4 = W(l, "lcw").rearrange("p (a b) -> p a b", a=2)
                for j in range(LRU_W):
                    for ct in range(2):
                        if j:
                            do(V.scalar_tensor_tensor(xc[:, ct, :], xlp[:, ct, j:j + S], lw4[:, ct, j:j + 1],
                                                      xc[:, ct, :], ALU.mult, ALU.add),
                               "lru_conv" if ct and j == LRU_W - 1 else "dve_steps")
                        else:
                            do(ts(xc[:, ct, :], xlp[:, ct, 0:S], lw4[:, ct, 0:1], W(l, "lcb")[:, ct:ct + 1],
                                  ALU.mult, ALU.add))
                b = full()
                for ct in range(2):
                    do(V.scalar_tensor_tensor(cacc[:, ct, :], b[:, 0:S], -1.0 / D_CONV, cacc[:, ct, :],
                                              ALU.mult, ALU.add), "dve_free" if ct else "dve_steps")
                do(V.tensor_tensor(csq, cacc[:, :, :], cacc[:, :, :], ALU.mult), "conv_sq")
                wait("lru_at")
                do(V.tensor_tensor(thr, av, av, ALU.mult))
                do(V.scalar_tensor_tensor(thr, thr, 1.0, tv, ALU.add, ALU.mult), "lru_q")
                do(ts(thi, thi, 0.5, 0.5, ALU.mult, ALU.add))
                do(V.tensor_tensor(thi, thi, xc, ALU.mult))
                wait("lru_root")
                do(V.tensor_tensor(thi, thi, thr, ALU.mult))
                for ct in range(2):
                    do(V.tensor_tensor_scan(xc[:, ct, :], av[:, ct, :], thi[:, ct, :], 0.0, ALU.mult, ALU.add))
                do(V.tensor_tensor(xc, xc, glg, ALU.mult))
                do(V.tensor_tensor(thr, xc, xc, ALU.mult), "lru_sq")
                if l == 0:
                    wait("trig")
                for lo, hi in ((0, 2), (2, 4), (4, 6), (6, 7)):
                    w = hi - lo
                    b = full()
                    pa = ropa[:, 0:w * S].rearrange("p (a b) -> p a b", a=w)
                    pb = ropb[:, 0:w * S].rearrange("p (a b) -> p a b", a=w)
                    step(V.tensor_tensor(pa, b[:, 0:w * S].rearrange("p (a b) -> p a b", a=w),
                                         sinT[:, :].unsqueeze(1).to_broadcast([P, w, S]), ALU.mult), "dve_free")
                    do(V.tensor_tensor(pb, raw[:, lo:hi, :], cosT[:, :].unsqueeze(1).to_broadcast([P, w, S]),
                                       ALU.mult))
                    do(V.tensor_tensor(raw[:, lo:hi, :], pa, pb, ALU.add), "rope_ready" if hi == 7 else "dve_steps")
                wait_drained("conv_sd", l)
                do(V.reciprocal(crs, crs))
                do(V.tensor_tensor(cacc[:, :, :], cacc[:, :, :], crs.unsqueeze(1).to_broadcast([P, 2, S]),
                                   ALU.mult), "conv_ln")
                gn = W(l, "gn")
                wait_drained("lru_rms", l)
                do(V.reciprocal(lrs, lrs))
                for ct in range(2):
                    do(V.scalar_tensor_tensor(yT[:, ct, :], xc[:, ct, :], gn[:, ct:ct + 1], lrs,
                                              ALU.mult, ALU.mult), "y_ready" if ct else "dve_steps")
                for h in range(NKV):
                    b = full()
                    for kv in range(2):
                        src = b[:, kv * S:(kv + 1) * S].rearrange("p (m s r) -> p m s r", s=CMP_STRIDE // 2, r=2)
                        pos = W(l, "posk" if kv == 0 else "posv")
                        for r in range(2):
                            lo, hi = r * HD, (r + 1) * HD
                            for a in range(2):
                                step(V.tensor_tensor(
                                    blkG[lo:hi, kv, 8 * a:8 * a + 8, h, :],
                                    src[lo:hi, a:a + NCMP, :, r].rearrange("p n s -> p s n"),
                                    pos[lo:hi, 8 * a:8 * a + 8].unsqueeze(2).to_broadcast([HD, 8, NCMP]), ALU.add),
                                     "dve_free" if kv and r and a else "dve_steps")
                wait("conv_silu")
                do(V.tensor_tensor(csq, cacc[:, :, :], cacc[:, :, :], ALU.mult), "conv_sq2")
                wait("gate_th")
                do(ts(gates[:, :, :, :], gates[:, :, :, :], 0.5, 0.5, ALU.mult, ALU.add))
                wait_drained("conv_rms", l)
                do(V.reciprocal(crs2, crs2))
                for ct in range(2):
                    do(V.scalar_tensor_tensor(yT[:, 6 + ct, :], cacc[:, ct, :], gn[:, 6 + ct:7 + ct], crs2,
                                              ALU.mult, ALU.mult), "y_ready" if ct else "dve_steps")
                b = full()
                do(V.tensor_copy(vcmp[:, :, :], b[0:NCMP, 0:NKV * HD].rearrange("p (a b) -> p a b", a=NKV)),
                   "dve_free")
                b = full()
                R = NH * NCMP
                do(V.tensor_tensor(vblk[:, :, :], b[0:R, 0:HD].unsqueeze(1).to_broadcast([R, NH, HD]),
                                   C("blk", R).unsqueeze(2).to_broadcast([R, NH, HD]), ALU.mult), "dve_free")

                mod_cols(l, 2)
                for t in range(TT):
                    attention(l, t)
                for t in range(TT):
                    wait("att_root")
                    do(V.reciprocal(astat[:, t, 2:3], astat[:, t, 1:2]))
                    do(ts(oatt[t], oatt[t], astat[:, t, 2:3], None, ALU.mult), "att_n")
                for t in range(TT):
                    b = full()
                    do(V.tensor_tensor(yT[:, 2:6, t * P:(t + 1) * P], b[:, :].rearrange("p (a b) -> p a b", a=4),
                                       gn[:, 2:6].unsqueeze(2).to_broadcast([P, 4, P]), ALU.mult), "dve_free")
                mod_cols(l, 3)
                gain_cols(l, 1, "n2g")
                wait_drained("row", l, 2, 1)
                for h in range(2):
                    for t in range(TT):
                        b = full()
                        dst = x[:, t, h * CH:(h + 1) * CH]
                        do(V.tensor_tensor(ropa, b[:, :], grow[:, h * CH:(h + 1) * CH], ALU.mult), "dve_free")
                        do(V.tensor_tensor(dst, dst, ropa, ALU.add), "x_done" if h and t else "dve_steps")
                normalize_rows()
                rows_to_hT(1)

                def tg(lo):
                    return rt[:, lo:lo + TT * NG].rearrange("p (t g) -> p t g", t=TT)

                def tv2(lo):
                    return rt[:, lo:lo + TT]

                def bc(ap):
                    return ap.unsqueeze(2).to_broadcast([P, TT, NG])

                def row4(name):
                    return C(name).unsqueeze(1).to_broadcast([P, TT, NG])

                def first_max(scores, top, onehot, scratch, index):
                    do(V.tensor_reduce(top, scores, X, ALU.max))
                    do(V.tensor_tensor(scratch, scores, bc(top), ALU.is_ge))
                    do(V.scalar_tensor_tensor(scratch, scratch, -1000.0, row4("gfar"), ALU.mult, ALU.add))
                    do(V.tensor_reduce(index, scratch, X, ALU.min))
                    do(V.tensor_tensor(onehot, row4("gidx"), bc(index), ALU.is_equal))

                if l < L - 1:
                    mod_cols(l + 1, 0)
                    mod_cols(l + 1, 1)
                lg = rt[:, 8:8 + TT * NR].rearrange("p (t n) -> p t n", t=TT)
                b = full()
                do(V.tensor_tensor(lg, b[:, 0:TT * NR].rearrange("p (t n) -> p t n", t=TT),
                                   W(l, "rb").unsqueeze(1).to_broadcast([P, TT, NR]), ALU.add), "dve_free")
                first_max(lg[:, :, 0:NG], tv2(48), tg(0), tg(50), gsel)
                do(V.tensor_tensor(tg(50), lg[:, :, 0:NG], bc(tv2(48)), ALU.subtract))
                do(V.tensor_copy(tg(180), tg(0)), "lg_ready")
                prod = rt[:, 80:112].rearrange("p (t g e) -> p t g e", t=TT, g=NG)
                for t in range(TT):
                    do(V.tensor_tensor(prod[:, t, :, :], lg[:, t, NG:].rearrange("p (g e) -> p g e", g=NG),
                                       tg(0)[:, t, :].unsqueeze(2).to_broadcast([P, NG, NE]), ALU.mult))
                    do(V.tensor_reduce(tg(72)[:, t, :], prod[:, t, :, :].rearrange("p g e -> p e g"), X, ALU.add))
                first_max(tg(72), tv2(112), tg(114), tg(188), tv2(196))
                do(V.scalar_tensor_tensor(tg(122), tg(114), NEG, tg(72), ALU.mult, ALU.add))
                first_max(tg(122), tv2(130), tg(132), tg(188), tv2(196))
                do(V.tensor_tensor(tv2(140), tv2(130), tv2(112), ALU.subtract), "top_d")
                b = full()
                do(V.tensor_tensor(tg(150), b[:, 0:2 * NG].rearrange("p (t g) -> p t g", t=TT), tg(0), ALU.mult))
                do(V.tensor_reduce(own1, tg(150), X, ALU.add))
                do(ts(own1, own1, 1.0, None, ALU.add))
                do(ts(rt[:, 164:168], b[:, 2 * NG:3 * NG], float(P), None, ALU.is_gt), "dve_free")
                do(V.tensor_reduce(rt[:, 168:169], rt[:, 164:168], X, ALU.max))
                do(V.tensor_tensor(rt[:, 160:164], rt[:, 164:168], C("gidx"), ALU.mult))
                do(V.tensor_reduce(rt[:, 169:170], rt[:, 160:164], X, ALU.add))
                do(V.tensor_copy(flag[:, :], rt[0:1, 168:170]), "routed")
                wait("lg_exp")
                do(V.tensor_reduce(tv2(68), tg(60), X, ALU.add))
                do(V.reciprocal(tv2(170), tv2(68)))
                wait("top_exp")
                do(ts(tv2(144), tv2(142), 1.0, None, ALU.add))
                do(V.reciprocal(tv2(146), tv2(144)))
                do(V.tensor_tensor(tv2(148), tv2(142), tv2(146), ALU.mult))
                do(V.tensor_tensor(tg(114), tg(114), bc(tv2(146)), ALU.mult))
                do(V.tensor_tensor(tg(132), tg(132), bc(tv2(148)), ALU.mult))
                do(V.tensor_tensor(tg(114), tg(114), tg(132), ALU.add))
                do(V.tensor_tensor(we[:, :, :], tg(114), bc(tv2(170)), ALU.mult))
                do(V.memset(gcur[:, 0:1], 0.0))
                select_tokens()
                wait_drained("row", l, 5, 1)
                if l < L - 1:
                    gain_cols(l + 1, 0, "n1g")

                with vec.Fori(0, NG) as g:
                    n.loop(g, TURNS)
                    made.loop(g, TURNS)
                    moe_pass(q, n, made, l, "loop")
                    n.end(NG)
                    made.end(NG)
                more = vec.value_load(flag[0:1, 0:1], min_val=0, max_val=1)
                with vec.If(more > 0):
                    m2, made2 = second[l], Waits()
                    credits(m2)
                    made2("dve_free", 3)

                    def do2(ins, name="dve_steps"):
                        ins.then_inc(m2[name], 1)
                        vec.wait_ge(m2[name], made2(name))

                    do2(V.tensor_copy(gcur[:, 0:1], rt[:, 169:170]))
                    do2(ts(own1, own1, -float(P), None, ALU.add))
                    do2(ts(gcur[:, 1:3], gsel, gcur[:, 0:1], None, ALU.is_equal))
                    do2(V.tensor_tensor(gcur[:, 3:5], gcur[:, 1:3], own1, ALU.mult))
                    for t in range(TT):
                        do2(ts(sel[:, t, :], C("iota"), gcur[:, 3 + t:4 + t], None, ALU.is_equal),
                            "sel_ready" if t == TT - 1 else "dve_steps")
                    moe_pass(m2, Waits(), made2, l, "second")
                do(V.memset(gcur[:, 0:1], 0.0), "x_done")

            wait("norm_root")
            vec.wait_ge(q["gain_in"], 16)
            do(V.reciprocal(stat[:, 4:6], stat[:, 2:4]))
            for t in range(TT):
                do(V.scalar_tensor_tensor(xn[:, t, :], x[:, t, :], stat[:, 4 + t:5 + t], acc[:, 1, :],
                                          ALU.mult, ALU.mult), "out_ready")

        @block.gpsimd
        def _(pool):
            made = Waits()
            made("acc_ready", 2)

            def do(ins, name="pool_steps"):
                ins.then_inc(q[name], 1)
                pool.wait_ge(q[name], made(name))

            def modulation(l, part, names, last_use):
                pool.wait_ge(*last_use)
                for h, (ring_l, name) in enumerate(names):
                    s, before = place(ring_l, name)
                    pool.wait_ge(loaded[s], 16 * (before + 1))
                    w = k3(ring[s][:, :], KD)
                    add = nc.gpsimd.tensor_tensor
                    do(add(w, w, sc[:, :].unsqueeze(2).to_broadcast([P, KD, CH]), ALU.mult))
                    do(add(w[:, 0:4, :], w[:, 0:4, :], w[:, 4:8, :], ALU.add))
                    do(add(w[:, 0:2, :], w[:, 0:2, :], w[:, 2:4, :], ALU.add))
                    sig = "acc_ready" if h else "pool_steps"
                    do(add(acc[:, (6 * l + part) % 3, h * CH:(h + 1) * CH], w[:, 0, :], w[:, 1, :], ALU.add), sig)
                    used["head", ring_l, name] = (sig, made.n[sig])

            pool.wait_ge(q["sc_ready"], 1)
            for l in range(L):
                for part in range(2, 6):
                    last_use = {2: ("acc_read", 2 * l), 3: written["cols", l, 0], 4: written["cols", l, 1],
                                5: ("acc_read", 2 * l + 1)}[part]
                    if part == 2 and l == 0:
                        last_use = ("sc_ready", 1)
                    modulation(l, part, [(l, "ada" + str(2 * part + h)) for h in range(2)], sem_at(q, last_use))
                if l < L - 1:
                    for part in range(2):
                        modulation(l + 1, part, [(l, "next" + str(2 * part + h)) for h in range(2)],
                                   sem_at(q, written["cols", l, 3 + part]))

        @block.sync
        def _(sync):
            def source(l, name):
                kind = name.rstrip("0123456789")
                if kind == "next":
                    l, kind, name = l + 1, "ada", "ada" + name[4:]
                if kind == "ada":
                    c = CH * int(name[3:])
                    return d["ada_w"][l].rearrange("(p k) n -> p k n", k=KD)[:, :, c:c + CH]
                if kind == "cmpk" or kind == "cmpv":
                    w1 = d["cmp_k_w1"] if kind == "cmpk" else d["cmp_v_w1"]
                    return w1[l].rearrange("(k p) n -> p k n", p=P)
                if kind == "out":
                    c = CH * int(name[3:])
                    return d["w_out"][l].rearrange("(k p) n -> p k n", p=P)[:, :, c:c + CH]
                lo, hi = {"conv": C_CONV, "lru": C_LRU, "q": C_Q, "kv": C_KV, "win": C_WIN}[kind]
                return d["w_in"][l].rearrange("(p k) n -> p k n", k=KD)[:, :, lo:hi]

            def load(l, name):
                s = place(l, name)[0]
                src = source(l, name)
                k, w = src.shape[1], src.shape[2]
                sync.dma_start(k3(ring[s][:, 0:k * w], k), src).then_inc(loaded[s], 16)

            def load_expert(l, name, g, sem):
                src = EX[name[0]][bass.ds(g * NE + (l * NG * NE + int(name[1])), 1), :, :]
                sync.dma_start(ring[place(l, name)[0]][:, :], src.rearrange("a p n -> p (a n)")).then_inc(sem, 16)

            sync.dma_start(scin[:, :], d["c"]).then_inc(q["c_in"], 16)
            load(0, "ada0")
            load(0, "ada1")
            sync.dma_start(posi[:, :], d["positions"]).then_inc(q["x_in"], 16)
            sync.dma_start(const[:, :], d["consts"]).then_inc(q["consts"], 16)
            sync.dma_start(x[:, :, :], d["x"].rearrange("a (t p) n -> p (a t) n", p=P)).then_inc(q["x_in"], 16)
            for l in range(L):
                sync.dma_start(param[l][:, :], d["params"][l]).then_inc(q["consts"], 16)
            first, rest = GROUP[:NSLOT], GROUP[NSLOT:]
            for l in range(L):
                head = HEADS[l]
                for i, name in enumerate(head):
                    if l == 0 and i < 2:
                        continue
                    if i >= NSLOT:
                        sync.wait_ge(*sem_at(q, used["head", l, head[i - NSLOT]]))
                    elif l:
                        sync.wait_ge(*sem_at(q, used["loop", l - 1, rest[i]], NG - 1))
                    load(l, name)
                for i, name in enumerate(first):
                    sync.wait_ge(*sem_at(q, used["head", l, head[i - NSLOT]]))
                    load_expert(l, name, 0, loaded[place(l, name)[0]])
                with sync.Fori(0, NG - 1) as g:
                    for name, last in zip(rest, first):
                        sync.wait_ge(*sem_at(q, used["loop", l, last], g))
                        load_expert(l, name, g, loaded[place(l, name)[0]])
                    for name, last in zip(first, rest):
                        sync.wait_ge(*sem_at(q, used["loop", l, last], g))
                        load_expert(l, name, g + 1, loaded[place(l, name)[0]])
                for name, last in zip(rest, first):
                    sync.wait_ge(*sem_at(q, used["loop", l, last], NG - 1))
                    load_expert(l, name, NG - 1, loaded[place(l, name)[0]])
                sync.wait_ge(q["routed"], l + 1)
                full = sync.value_load(flag[0:1, 0:1], min_val=0, max_val=1)
                with sync.If(full > 0):
                    g2 = sync.value_load(flag[0:1, 1:2], min_val=0, max_val=NG - 1)
                    for name in rest:
                        sync.wait_ge(*sem_at(q, used["loop", l, name], NG - 1))
                    for j, name in enumerate(GROUP):
                        if j >= 3:
                            sync.wait_ge(*sem_at(second[l], used["second", l, GROUP[j - 3]]))
                        load_expert(l, name, g2, loaded2[l][j % 3])
                    for name in GROUP[-3:]:
                        sync.wait_ge(*sem_at(second[l], used["second", l, name]))
            for t in range(TT):
                sync.wait_ge(q["out_ready"], t + 1)
                sync.dma_start(out[0, t * P:(t + 1) * P, :], xn[:, t, :]).then_inc(q["stored"], 16)
            sync.wait_ge(q["stored"], 16 * TT)


INS = ("moe_w_gate", "moe_w_up", "moe_w_down", "ada_w", "ada_b", "w_in", "w_out", "cmp_k_w1", "cmp_v_w1", "x")


def kernel(**inputs):
    import concourse.bacc as bacc
    from concourse.bass_utils import run_bass_kernel_spmd

    a = {k: np.ascontiguousarray(v) for k, v in inputs.items()}
    nc = bacc.Bacc("TRN2", target_bir_lowering=False, num_devices=1)

    def dcol(v):
        return v.reshape(P, KD)

    def ccol(v):
        return v.reshape(-1, P).T

    params = np.zeros((L, P, NPARAM), np.float32)
    for l in range(L):
        def put(name, v):
            lo, hi = PARAM[name]
            params[l, :, lo:hi] = v.reshape(P, hi - lo)

        put("n1g", dcol(a["norm1_g"][l]))
        put("n2g", dcol(a["norm2_g"][l]))
        put("adab", np.concatenate([dcol(a["ada_b"][l, i * D:(i + 1) * D]) for i in (0, 1, 3, 4)], 1))
        put("lcw", a["lru_conv_w"][l].reshape(LRU_W, 2, P).transpose(2, 1, 0))
        put("lcb", ccol(a["lru_conv_b"][l]))
        put("ba", ccol(a["lru_ba"][l]))
        put("bx", ccol(a["lru_bx"][l]))
        put("lam", ccol(a["lru_lambda"][l]))
        put("ccw", a["cnv_dw_w"][l].reshape(CONV_K, 2, P).transpose(2, 1, 0))
        put("ccb", ccol(a["cnv_dw_b"][l]))
        put("lng", ccol(a["cnv_ln_g"][l]))
        put("lnb", ccol(a["cnv_ln_b"][l]))
        put("gn", ccol(a["out_norm_g"][l]))
        rb = np.concatenate([a["moe_rg_b"][l], a["moe_re_b"][l].reshape(-1)])
        put("rb", np.broadcast_to(rb, (P, NR)))
        for name, src in (("posk", "cmp_pos_k"), ("posv", "cmp_pos_v")):
            put(name, a[src][l].reshape(LP, P).T)
        for name, src in (("wa", "lru_wa"), ("wx", "lru_wx")):
            w = np.zeros((P, 2, P), np.float32)
            for i in range(4):
                o = 64 * (i % 2)
                w[o:o + 64, i // 2, o:o + 64] = a[src][l, i]
            put(name, w)
        rw = np.concatenate([a["moe_rg_w"][l], a["moe_re_w"][l].transpose(1, 0, 2).reshape(D, NG * NE)], 1)
        put("rw", rw)
        w2 = a["cmp_k_w2"][l].reshape(2, P, HD).transpose(1, 0, 2)
        put("w2k", np.concatenate([w2, w2], 2))
        put("w2v", a["cmp_v_w2"][l].reshape(2, P, HD).transpose(1, 0, 2))

    arrays = {k: a[k] for k in INS}
    arrays["params"] = params
    arrays["consts"] = constants()
    arrays["c"] = dcol(a["c"][0])
    arrays["positions"] = np.ascontiguousarray(np.broadcast_to(a["positions"], (P, S)))
    arrays["final_norm_g"] = np.ascontiguousarray(np.broadcast_to(a["final_norm_g"], (P, D)))
    d = {}
    feeds = {}
    for name, v in arrays.items():
        v = np.ascontiguousarray(v)
        feeds[name + "_in"] = v
        d[name] = nc.dram_tensor(name + "_in", v.shape, mybir.dt.from_np(v.dtype), kind="ExternalInput").ap()
    out = nc.dram_tensor("out", (1, S, D), mybir.dt.float32, kind="ExternalOutput").ap()
    build(nc, d, out)
    r = run_bass_kernel_spmd(nc, [feeds], core_ids=[0])
    return r.results[0]["out"]
```

```python
import numpy as np
import concourse.bass as bass
from concourse import mybir
from contextlib import ExitStack

P = 128
D = 1024
S = 256
TT = S // P
L = 2
KD = D // P
D_LRU, D_ATT, D_CONV = 256, 512, 256
HD, NH, NKV = 64, 8, 2
GQA = NH // NKV
CMP_LEN, CMP_STRIDE, CMP_HID = 32, 16, 256
NCMP = (S - CMP_LEN) // CMP_STRIDE + 1
LRU_W, CONV_K = 4, 31
NG, NE, FH = 4, 4, 512
EPS = 1e-6
NEG = -1e30
THETA = 10000.0
LP = CMP_LEN * HD // P
CH = 512
SLOT = 4096
NSLOT = 4
QT = SLOT // 4
NQ = 3
NC6 = 6 * D
IN_COLS = 2328
C_CONV, C_LRU, C_Q, C_KV, C_WIN = (1816, 2328), (0, 512), (512, 1024), (1024, 1536), (1536, 1816)


def layout(fields):
    at, out = 0, {}
    for name, n in fields:
        out[name] = (at, at + n)
        at += n
    return out, at


CONST, NCONST = layout([("ident", P), ("ones", P), ("causal", 2 * P), ("cmask", TT * NCMP), ("anyv", TT),
                        ("tri", P), ("iota", P), ("gidx", NG), ("gfar", NG), ("rot", P), ("dup", 2 * P),
                        ("rep", 2 * NH * NCMP), ("blk", NH), ("inv", 1), ("eps", 1)])
PARAM, NPARAM = layout([("n1g", KD), ("n2g", KD), ("adab", 4 * KD), ("lcw", 2 * LRU_W), ("lcb", 2), ("ba", 2),
                        ("bx", 2), ("lam", 2), ("ccw", 2 * CONV_K), ("ccb", 2), ("lng", 2), ("lnb", 2),
                        ("gn", KD), ("rb", NG + NG * NE), ("posk", LP), ("posv", LP), ("wa", 2 * P),
                        ("wx", 2 * P), ("rw", KD * (NG + NG * NE)), ("w2k", 2 * P), ("w2v", 2 * HD)])
NR = NG + NG * NE


def constants():
    c = np.zeros((P, NCONST), np.float32)

    def put(name, a, rows=P):
        lo, hi = CONST[name]
        c[:rows, lo:hi] = np.asarray(a, np.float32).reshape(rows, hi - lo)

    p = np.arange(P)
    eye = np.eye(P)
    put("ident", eye)
    put("ones", np.ones((P, P)))
    put("causal", np.concatenate([np.zeros((P, P)), np.where(p[None, :] <= p[:, None], 0.0, NEG)], 1))
    t = p[:, None] + P * np.arange(TT)[None, :]
    end = np.arange(NCMP) * CMP_STRIDE + CMP_LEN - 1
    valid = end[None, None, :] <= t[:, :, None]
    put("cmask", np.where(valid, 0.0, NEG))
    put("anyv", valid.any(-1))
    put("tri", p[:, None] < p[None, :])
    put("iota", np.tile(p + 1, (P, 1)))
    put("gidx", np.tile(np.arange(NG), (P, 1)))
    put("gfar", np.tile(np.arange(NG) + 1000, (P, 1)))
    rot = np.zeros((P, P))
    for m in range(P):
        if m % HD < HD // 2:
            rot[m + HD // 2, m] = -1
        else:
            rot[m - HD // 2, m] = 1
    put("rot", rot)
    dup = np.zeros((P, 2, P))
    for h in range(2):
        for m in range(P):
            dup[h * HD + m % HD, h, m] = 1
    put("dup", dup)
    rep = np.zeros((NCMP, 2, NH, NCMP))
    for h in range(NH):
        for n in range(NCMP):
            rep[n, h // GQA, h, n] = 1
    put("rep", rep, NCMP)
    blk = np.zeros((NH * NCMP, NH))
    for h in range(NH):
        blk[h * NCMP:(h + 1) * NCMP, h] = 1
    put("blk", blk, NH * NCMP)
    inv = np.float32(THETA) ** (-np.arange(0, HD, 2, dtype=np.float32) / np.float32(HD))
    put("inv", inv[p % (HD // 2)])
    put("eps", np.full(P, EPS))
    return c


class Waits:

    def __init__(self):
        self.n, self.turn, self.per, self.start = {}, None, {}, {}

    def __call__(self, name, by=1):
        self.n[name] = self.n.get(name, 0) + by
        return self.now(name)

    def now(self, name):
        if self.turn is None:
            return self.n[name]
        return self.turn * self.per[name] + self.n[name]

    def loop(self, turn, per):
        self.turn, self.per, self.start = turn, per, dict(self.n)

    def end(self, turns):
        for name, n in self.n.items():
            if n != self.start.get(name, 0):
                assert n - self.start.get(name, 0) == self.per[name], (name, n - self.start.get(name, 0))
                self.n[name] += (turns - 1) * self.per[name]
        self.turn = None


PASS_SEMS = ("act_full", "act_free", "dve_full", "dve_free", "dve_steps", "sel_ready", "ys_ready", "hi_ready",
             "lo_ready", "split_free", "operand_hi", "xg_ready")
QUARTERS = 4 * 3 * NE
TURNS = {"act_full": 2, "act_free": NE + 2, "dve_full": 2 + NE + 1 + 4, "dve_free": 2 + NE + NE + 1 + 4,
         "dve_steps": 5, "sel_ready": 1, "ys_ready": 2, "hi_ready": QUARTERS, "lo_ready": QUARTERS,
         "split_free": QUARTERS, "operand_hi": NE + 1, "xg_ready": 1}
TURNS["act_jobs"], TURNS["dve_jobs"] = TURNS["act_free"], TURNS["dve_free"]
SEMS = ("consts", "c_in", "x_in", "late_in", "sc_ready", "bias_row", "acc_ready", "acc_read", "modcols", "norm_root", "xn_ready",
        "conv_sum", "conv_sq", "conv_sd", "conv_ln", "conv_silu", "conv_sq2", "lru_conv", "lru_at", "lru_q",
        "lru_root", "lru_sq", "rope_ready", "gate_th", "cmp_s", "cmp_p", "s_ready", "p_ready", "pT_read",
        "o_free", "att_ss", "att_root", "att_n", "y_ready", "lg_ready", "lg_exp", "top_d", "top_exp",
        "routed", "lam_a", "lam_e", "lam_w", "lam_ln", "angle", "trig", "x_done", "act_steps", "gain_in",
        "out_ready", "stored", "pool_steps")

OWN = ("conv", "ada4", "lru", "ada5", "q", "kv", "win", "ada6", "ada7", "cmpk", "cmpv", "ada8", "ada9", "ada10",
       "ada11")
HEADS = [(("ada0", "ada1", "ada2", "ada3") if l == 0 else ()) + OWN +
         (("next0", "next1", "next2", "next3", "out0", "out1") if l < L - 1 else ("out0", "out1")) for l in range(L)]
GATHER = ((0, 1, 2), (3, 4, 5), (6, 7))
CMP = ("cmpk", "cmpv")
GROUP = ("g0", "u0", "g1", "u1", "d0", "g2", "u2", "d1", "g3", "u3", "d2", "d3")
BEFORE = [sum(len(HEADS[i]) + NG * len(GROUP) for i in range(l)) for l in range(L)]
TURN = len(GROUP) // NSLOT


def place(l, name):
    c = BEFORE[l] + (HEADS[l].index(name) if name in HEADS[l] else len(HEADS[l]) + GROUP.index(name))
    return c % NSLOT, c // NSLOT


def build(nc, d, out):
    f32, i32, f32r = mybir.dt.float32, mybir.dt.int32, mybir.dt.float32r
    ALU, ACT, X = mybir.AluOpType, mybir.ActivationFunctionType, mybir.AxisListType.X

    ctx = ExitStack()
    with ctx:
        def sb(name, shape, dt=f32):
            return ctx.enter_context(nc.sbuf_tensor(name, shape, dt))

        def sems(names, prefix=""):
            return {n: ctx.enter_context(nc.semaphore(prefix + n)) for n in names}

        ring = [sb(f"ring{i}", [P, SLOT]) for i in range(NSLOT)]
        const = sb("const", [P, NCONST])
        param = [sb(f"param{l}", [P, NPARAM]) for l in range(L)]
        x = sb("x", [P, TT, D])
        xn = sb("xn", [P, TT, D])
        hT = sb("hT", [P, KD, S])
        yT = sb("yT", [P, KD, S])
        acc = sb("acc", [P, 3, D])
        grow = sb("grow", [P, D])
        cols = sb("cols", [P, 4, KD])
        amul = sb("amul", [P, 2, KD])
        scin = sb("scin", [P, KD])
        sc = sb("sc", [P, KD])
        stat = sb("stat", [P, 8])
        astat = sb("astat", [P, TT, 3])
        posi = sb("posi", [P, S], i32)
        cosT = sb("cosT", [P, S])
        sinT = sb("sinT", [P, S])
        raw = sb("raw", [P, 7, S])
        kcat = sb("kcat", [P, NKV, 2, S])
        vslc = sb("vslc", [P, TT, P])
        vwin = sb("vwin", [P, TT, P + 3 * NH])
        gates = sb("gates", [P, TT, NH, 3])
        hidc = sb("hidc", [P, 2, 2, NKV * NCMP])
        kcmp = sb("kcmp", [P, NKV * NCMP])
        vcmp = sb("vcmp", [NCMP, NKV, HD])
        xlp = sb("xlp", [P, 2, LRU_W - 1 + S])
        vp = sb("vp", [P, 2, CONV_K - 1 + S])
        vblk = vp[:, :, :].rearrange("p a b -> p (a b)")[0:NH * NCMP, 0:NH * HD].rearrange("p (h e) -> p h e", h=NH)
        wh = [sb(f"wh{i}", [P, QT], f32r) for i in range(NQ)]
        wl = [sb(f"wl{i}", [P, QT], f32r) for i in range(NQ)]
        xgh, xgl = (sb(name, [P, KD, P], f32r) for name in ("xgh", "xgl"))
        hidTh, hidTl = ([sb(f"{name}{i}", [P, FH], f32r) for i in range(2)] for name in ("hidTh", "hidTl"))
        cacc = sb("cacc", [P, 2, S])
        lamb = sb("lamb", [P, L, 6])
        ltmp = sb("ltmp", [P, L, 12])
        mx = sb("mx", [P, NH, 4])
        sums = sb("sums", [P, TT, 3, NH])
        coef = sb("coef", [P, TT, 3, NH])
        cmx = sb("cmx", [P, NH])
        we = sb("we", [P, TT, NE])
        rt = sb("rt", [P, 256])
        flag = sb("flag", [1, 2], i32)
        sel = sb("sel", [P, TT, P])
        selT = sb("selT", [P, TT, P])
        wslot = sb("wslot", [P, NE])
        gcur = sb("gcur", [P, 8])
        arena = sb("arena", [P, 3072])
        silu = [arena[:, 0:512], arena[:, 512:1024]]
        hid = [arena[:, 1024:1536], arena[:, 1536:2048]]
        xg = arena[:, 2048:3072].rearrange("p (k c) -> p k c", c=P)
        ys = raw[:, 0:4, :].rearrange("p a b -> p (a b)")
        brow = {2: hT[0:1, 0:4, :].rearrange("p a b -> p (a b)"), 5: arena[0:1, 2 * D:3 * D]}
        sp = [xn[:, i // 2, 512 * (i % 2):512 * (i % 2) + 512] for i in range(4)]
        pT = [arena[:, 512 * i:512 * (i + 1)] for i in range(4)]
        oatt = [hT[:, 2 * t:2 * t + 2, :].rearrange("p a b -> p (a b)") for t in range(TT)]
        otmp = hT[:, 6:8, :].rearrange("p a b -> p (a b)")
        scmp = hT[:, 4, 0:NH * NCMP]
        pcT = hT[:, 5, 0:P]
        xc, thr, thi, av = (xn[:, i // 2, 512 * (i % 2):512 * (i % 2) + 512].rearrange("p (a b) -> p a b", a=2)
                            for i in range(4))
        tv = yT[:, 2:4, :]
        cu, cth, csq = (arena[:, 512 * i:512 * (i + 1)].rearrange("p (a b) -> p a b", a=2) for i in range(3))
        crs, crs2 = arena[:, 1536:1792], arena[:, 1792:2048]
        vcT = arena[:, 2048:2304]
        glg = arena[:, 2304:2816].rearrange("p (a b) -> p a b", a=2)
        lrs = arena[:, 2816:3072]
        hidr = arena[:, 2304:2304 + CMP_HID]
        ropa, ropb = arena[:, 0:512], arena[:, 512:1024]
        blkG = arena[:, 0:2 * LP * NKV * NCMP].rearrange("p (v k h n) -> p v k h n", v=2, k=LP, h=NKV)
        bank = [ctx.enter_context(nc.psum_tensor(f"bank{i}", [P, 512], f32)) for i in range(8)]
        opsum = bank[6:8]

        q = sems(SEMS + PASS_SEMS)
        second = [sems(PASS_SEMS, f"second{l}_") for l in range(L)]
        loaded = [ctx.enter_context(nc.semaphore(f"loaded{i}")) for i in range(NSLOT)]
        loaded2 = [[ctx.enter_context(nc.semaphore(f"second{l}_loaded{i}")) for i in range(3)] for l in range(L)]

        def C(name, rows=P):
            return const[:rows, CONST[name][0]:CONST[name][1]]

        def W(l, name):
            return param[l][:, PARAM[name][0]:PARAM[name][1]]

        def abank(k):
            return bank[(k - 1) % 3]

        def dbank(k):
            return bank[3 + (k - 1) % 3]

        ident, ones = C("ident"), C("ones")
        wg_v = d["moe_w_gate"].rearrange("l g e (p k) f -> (l g e) p (k f)", k=KD)
        wu_v = d["moe_w_up"].rearrange("l g e (p k) f -> (l g e) p (k f)", k=KD)
        wd_v = d["moe_w_down"].rearrange("l g e (p k) f -> (l g e) p (k f)", k=FH // P)
        EX = {"g": wg_v, "u": wu_v, "d": wd_v}

        def k3(ap, k):
            return ap.rearrange("p (k n) -> p k n", k=k)

        def slot_of(l, name):
            return ring[place(l, name)[0]]

        block = ctx.enter_context(nc.Block())

        written, drained, used, bank_of = {}, {}, {}, {}

        def sem_at(m, mark, turn=None, back=0):
            name, value = mark
            if turn is None:
                return m[name], value
            return m[name], turn * TURNS[name] + (value - back * TURNS[name])

        @block.tensor
        def _(pe):
            n = Waits()
            mm = nc.tensor.matmul

            def proj_ch(b, l, name, c0, tiles, at=0):
                w = k3(slot_of(l, name)[:, :], KD) if name != "win" else \
                    k3(slot_of(l, name)[:, 0:KD * (C_WIN[1] - C_WIN[0])], KD)
                for i in range(tiles):
                    for k in range(KD):
                        last = mm(b[:, at + i * S:at + (i + 1) * S], w[:, k, c0 + i * P:c0 + (i + 1) * P],
                                  hT[:, k, :], start=(k == 0), stop=(k == KD - 1))
                return last

            def proj_tok(b, l, name, c0, width):
                w = k3(slot_of(l, name)[:, :], KD) if name != "win" else \
                    k3(slot_of(l, name)[:, 0:KD * (C_WIN[1] - C_WIN[0])], KD)
                for t in range(TT):
                    for k in range(KD):
                        last = mm(b[:, t * width:(t + 1) * width], hT[:, k, t * P:(t + 1) * P],
                                  w[:, k, c0:c0 + width], start=(k == 0), stop=(k == KD - 1))
                return last

            def arrived(l, name):
                s, before = place(l, name)
                pe.wait_ge(loaded[s], 16 * (before + 1))

            def job(which, key, m, n, signalled):
                full, free = which + "_full", which + "_free"
                pe.wait_ge(m[free], n(free))
                if signalled:
                    n(full)
                    written[key] = full, n.n[full]
                k = n.n[free]
                drained[key] = free, k + 3
                bank_of[key] = abank(k) if which == "act" else dbank(k)
                return bank_of[key]

            def act_job(*key, m=q, n=n, signalled=True):
                return job("act", key, m, n, signalled)

            def dve_job(*key, m=q, n=n, signalled=True):
                return job("dve", key, m, n, signalled)

            def wait_drained(*key, m=q, n=n):
                pe.wait_ge(*sem_at(m, drained[key], n.turn))

            def mod_cols(l, part):
                b = dve_job("cols", l, part)
                pe.wait_ge(q["acc_ready"], 6 * l + part + 1)
                for k in range(KD):
                    last = mm(b[:, k:k + 1], acc[:, (6 * l + part) % 3, k:D:KD], ones[:, 0:1], start=True, stop=True)
                last.then_inc(q["dve_full"], 1)

            def mod_row(part, l):
                pe.wait_ge(q["acc_ready"], 6 * l + part + 1)
                pe.wait_ge(q["bias_row"], n("bias_row", 16))
                for h in range(2):
                    b = act_job("row", l, part, h)
                    last = mm(b[:, :], ones, acc[:, (6 * l + part) % 3, h * CH:(h + 1) * CH], start=True, stop=False)
                    if h:
                        last.then_inc(q["acc_read"], 1)
                    last = mm(b[:, :], C("ones", 1), brow[part][:, h * CH:(h + 1) * CH], start=False, stop=True)
                    last.then_inc(q["act_full"], 1)

            def rows_to_hT(l, norm):
                pe.wait_ge(q["xn_ready"], n("xn_ready"))
                for j in range(KD // 2):
                    b = act_job("hT", l, norm, j) if j % 2 == 0 else dve_job("hT", l, norm, j)
                    for i in range(2):
                        for t in range(TT):
                            last = nc.tensor.transpose(b[:, i * S + t * P:i * S + (t + 1) * P],
                                                       xn[:, t, 2 * j + i:D:KD], ident)
                    last.then_inc(q["act_full" if j % 2 == 0 else "dve_full"], 1)
                wait_drained("hT", l, norm, 2)
                wait_drained("hT", l, norm, 3)

            def sum_rows(b, src, last_sem):
                for ct in range(2):
                    last = mm(b[:, 0:S], ones, src[:, ct, :], start=(ct == 0), stop=(ct == 1))
                last.then_inc(q[last_sem], 1)

            def compressed(l, t):
                b = dve_job("ocmp", l, t)
                wait_drained("pcT", l, t)
                mm(b[:, :], pcT[0:NH * NCMP, :], vblk[:, :, :].rearrange("p a b -> p (a b)"),
                   start=True, stop=True).then_inc(q["dve_full"], 1)

            def attention(l, t):
                V = (vslc, vwin)
                nb = t + 1

                def query(h):
                    o = HD * (h % 2)
                    return raw[o:o + HD, h // 2, t * P:(t + 1) * P], o, h // GQA

                for par in range(2):
                    b = dve_job("scmp", l, t, par)
                    for h in range(par, NH, 2):
                        qh, o, g = query(h)
                        last = mm(b[:, h * 16:h * 16 + NCMP], qh, kcmp[o:o + HD, g * NCMP:(g + 1) * NCMP],
                                  start=True, stop=True)
                    last.then_inc(q["dve_full"], 1)
                for i in range(NH // 2 + 2):
                    if i < NH // 2:
                        pair = [(h, dve_job("scores", l, t, h)) for h in (2 * i, 2 * i + 1)]
                        for h, b in pair:
                            qh, o, g = query(h)
                            mm(b[:, :].rearrange("p (a b) -> p a b", a=2)[:, :, 0:nb * P], qh,
                               kcat[o:o + HD, g, :, 0:nb * P], start=True, stop=True).then_inc(q["dve_full"], 1)
                    if i == 0 and t:
                        compressed(l, t - 1)
                    if i == 1:
                        b = act_job("pcT", l, t)
                        pe.wait_ge(q["cmp_p"], n("cmp_p"))
                        nc.tensor.transpose(b[0:NH * NCMP, 0:P], scmp, ident).then_inc(q["act_full"], 1)
                    if 1 <= i <= NH // 2:
                        for h in (2 * i - 2, 2 * i - 1):
                            key = ("pT", (l * TT + t) * NH + h)
                            b = act_job(*key) if h % 2 == 0 else dve_job(*key)
                            pe.wait_ge(q["p_ready"], n("p_ready"))
                            for ty in range(2):
                                for kb in range(nb):
                                    last = nc.tensor.transpose(b[:, (ty * nb + kb) * P:(ty * nb + kb + 1) * P],
                                                               sp[h % 4][:, ty * S + kb * P:ty * S + (kb + 1) * P],
                                                               ident)
                            last.then_inc(q["act_full" if h % 2 == 0 else "dve_full"], 1)
                    if i >= 2:
                        for h in (2 * i - 4, 2 * i - 3):
                            if h == 0 and (l or t):
                                pe.wait_ge(q["o_free"], n("o_free"))
                            wait_drained("pT", (l * TT + t) * NH + h)
                            for ty in range(2):
                                for kb in range(nb):
                                    last = mm(opsum[ty][:, h * HD:(h + 1) * HD],
                                              pT[h % 4][:, (ty * nb + kb) * P:(ty * nb + kb + 1) * P],
                                              V[ty][:, kb, (h // GQA) * HD:(h // GQA + 1) * HD],
                                              start=(kb == 0), stop=(kb == nb - 1))
                            last.then_inc(q["pT_read"], 1)
            def gather(m, n, l, kind):
                pe.wait_ge(m["sel_ready"], n("sel_ready"))
                for ks in GATHER:
                    ring_of, name = (dve_job, "dve_full") if ks is GATHER[-1] else (act_job, "act_full")
                    b = ring_of(kind, l, "gather", ks[0], m=m, n=n)
                    for i, k in enumerate(ks):
                        for t in range(TT):
                            last = mm(b[:, i * P:(i + 1) * P], xn[:, t, k:D:KD], sel[:, t, :],
                                      start=(t == 0), stop=(t == TT - 1))
                    last.then_inc(m[name], 1)

            def moe_pass(m, n, l, kind):
                def adrain(*key, signalled=True):
                    return act_job(kind, l, *key, m=m, n=n, signalled=signalled)

                def vdrain(*key, signalled=True):
                    return dve_job(kind, l, *key, m=m, n=n, signalled=signalled)

                def selection():
                    b = vdrain("weights")
                    for t in range(TT):
                        last = mm(b[:, 0:NE], sel[:, t, :], we[:, t, :], start=(t == 0), stop=(t == TT - 1))
                    last.then_inc(m["dve_full"], 1)
                    b = vdrain("selT")
                    for t in range(TT):
                        last = nc.tensor.transpose(b[:, t * P:(t + 1) * P], sel[:, t, :], ident)
                    last.then_inc(m["dve_full"], 1)

                def quarter(products):
                    i = n.n.get("hi_ready", 0) % NQ
                    pe.wait_ge(m["hi_ready"], n("hi_ready"))
                    for w, part in ((wh[i], 0), (wh[i], 1), (wl[i], 0)):
                        if w is wl[i]:
                            pe.wait_ge(m["lo_ready"], n("lo_ready"))
                        for dst, left, c, start, stop in products:
                            last = mm(dst, left[part], w[:, c:c + CH], start=start and w is wh[i] and part == 0,
                                      stop=stop and w is wl[i])
                    last.then_inc(m["split_free"], 1)
                    n("split_free")

                def up(c, e):
                    b = (adrain if c == "g" else vdrain)(c, e, signalled=False)
                    for i in range(4):
                        quarter([(b[:, :], (xgh[:, k, :], xgl[:, k, :]), (k % 2) * CH, k == 0, k == KD - 1)
                                 for k in (2 * i, 2 * i + 1)])
                    written[kind, l, c, e] = ("split_free", n.n["split_free"] + NQ)

                def transpose(e):
                    b = vdrain("hidT", e)
                    wait_drained(kind, l, "u", e, m=m, n=n)
                    for j in range(FH // P):
                        last = nc.tensor.transpose(b[:, j * P:(j + 1) * P], hid[e % 2][:, j:FH:FH // P], ident)
                    last.then_inc(m["dve_full"], 1)

                def down(e):
                    wait_drained(kind, l, "hidT", e, m=m, n=n)
                    for j in range(FH // P):
                        left = tuple(part[e % 2][:, j * P:(j + 1) * P] for part in (hidTh, hidTl))
                        quarter([(opsum[h][:, :], left, h * CH, e == 0 and j == 0, e == NE - 1 and j == FH // P - 1)
                                 for h in range(2)])
                    written[kind, l, "d", e] = ("split_free", n.n["split_free"] + NQ)

                pe.wait_ge(m["xg_ready"], n("xg_ready"))
                up("g", 0)
                selection()
                up("u", 0)
                up("g", 1)
                transpose(0)
                up("u", 1)
                down(0)
                up("g", 2)
                transpose(1)
                up("u", 2)
                down(1)
                up("g", 3)
                transpose(2)
                up("u", 3)
                down(2)
                transpose(3)
                if kind == "loop":
                    gather(m, n, l, kind)
                down(3)
                for h in range(2):
                    pe.wait_ge(m["ys_ready"], n("ys_ready"))
                    for t in range(TT):
                        b = vdrain("scatter", t, h)
                        mm(b[:, :], selT[:, t, :], ys[:, h * CH:(h + 1) * CH], start=True, stop=True)\
                            .then_inc(m["dve_full"], 1)

            pe.wait_ge(q["consts"], 32)
            mod_cols(0, 0)
            mod_cols(0, 1)
            for l in range(L):
                rows_to_hT(l, 0)
                arrived(l, "conv")
                for h in range(2):
                    last = proj_ch(act_job("conv", l, h), l, "conv", h * D_CONV, 2).then_inc(q["act_full"], 1)
                used["head", l, "conv"] = written["conv", l, 1]
                arrived(l, "lru")
                for h in range(2):
                    last = proj_ch(act_job("lru", l, h), l, "lru", h * D_LRU, 2).then_inc(q["act_full"], 1)
                used["head", l, "lru"] = written["lru", l, 1]
                arrived(l, "q")
                for h in range(2):
                    last = proj_ch(act_job("q", l, h), l, "q", h * 2 * P, 2).then_inc(q["act_full"], 1)
                used["head", l, "q"] = written["q", l, 1]
                arrived(l, "kv")
                b = act_job("kcks", l)
                proj_ch(b, l, "kv", 0, 1)
                proj_ch(b, l, "kv", 2 * P, 1, at=S).then_inc(q["act_full"], 1)
                proj_ch(act_job("vc", l), l, "kv", P, 1).then_inc(q["act_full"], 1)
                pe.wait_ge(q["lru_conv"], n("lru_conv"))
                for name in ("wa", "wx"):
                    b = act_job(name, l)
                    w = W(l, name).rearrange("p (a b) -> p a b", a=2)
                    for ct in range(2):
                        last = mm(b[:, ct * S:(ct + 1) * S], w[:, ct, :], xc[:, ct, :], start=True, stop=True)
                    last.then_inc(q["act_full"], 1)
                b = dve_job("conv_mean", l)
                pe.wait_ge(q["conv_sum"], n("conv_sum"))
                sum_rows(b, cacc, "dve_full")
                proj_tok(act_job("vs", l), l, "kv", 3 * P, P).then_inc(q["act_full"], 1)
                used["head", l, "kv"] = written["vs", l]
                arrived(l, "win")
                proj_ch(act_job("kw", l), l, "win", 0, 1).then_inc(q["act_full"], 1)
                proj_tok(act_job("vwin", l), l, "win", P, P + 3 * NH).then_inc(q["act_full"], 1)
                used["head", l, "win"] = written["vwin", l]
                wait_drained("kw", l)
                for lo, hi in ((0, 2), (2, 4), (4, 6), (6, 7)):
                    b = dve_job("rope", l, lo)
                    mm(b[:, 0:(hi - lo) * S], C("rot"), raw[:, lo:hi, :], start=True, stop=True)\
                        .then_inc(q["dve_full"], 1)
                b = act_job("conv_sd", l)
                pe.wait_ge(q["conv_sq"], n("conv_sq"))
                sum_rows(b, csq, "act_full")
                b = act_job("lru_rms", l)
                pe.wait_ge(q["lru_sq"], n("lru_sq"))
                sum_rows(b, thr, "act_full")
                mod_row(2, l)
                pe.wait_ge(q["rope_ready"], n("rope_ready"))
                dup = C("dup").rearrange("p (a b) -> p a b", a=2)
                for h in range(NKV):
                    b = act_job("kcat", l, h)
                    mm(b[:, :], dup[:, h, :], raw[:, 5:7, :], start=True, stop=True).then_inc(q["act_full"], 1)
                for h in range(NKV):
                    b = dve_job("blk", l, h)
                    mm(b[:, 0:S], dup[:, h, :], raw[:, 4, :], start=True, stop=True)
                    mm(b[:, S:2 * S], dup[:, h, :], vcT, start=True, stop=True).then_inc(q["dve_full"], 1)
                mod_cols(l, 3)
                b = act_job("conv_rms", l)
                pe.wait_ge(q["conv_sq2"], n("conv_sq2"))
                sum_rows(b, csq, "act_full")
                wait_drained("blk", l, 1)
                banks = [act_job(name, l) for name in CMP]
                for name in CMP:
                    arrived(l, name)
                for k in range(LP):
                    for kv, name in enumerate(CMP):
                        last = mm(banks[kv][32 * kv:32 * kv + NKV * NCMP, 0:CMP_HID],
                                  blkG[:, kv, k, :, :].rearrange("p a b -> p (a b)"),
                                  k3(slot_of(l, name)[:, :], LP)[:, k, :], start=(k == 0), stop=(k == LP - 1))
                        if k == LP - 1:
                            last.then_inc(q["act_full"], 1)
                            used["head", l, name] = written[name, l]
                for kv, name in enumerate(CMP):
                    b = act_job("hidc", l, kv)
                    wait_drained(name, l)
                    lo, hi = 32 * kv, 32 * kv + NKV * NCMP
                    for m_ in range(2):
                        last = nc.tensor.transpose(b[:, m_ * 32:m_ * 32 + NKV * NCMP],
                                                   hidr[lo:hi, m_ * P:(m_ + 1) * P], ident[lo:hi, lo:hi])
                    last.then_inc(q["act_full"], 1)
                wait_drained("hidc", l, 1)
                b = act_job("kcmp", l)
                w2 = W(l, "w2k").rearrange("p (a b) -> p a b", a=2)
                for m_ in range(2):
                    last = mm(b[:, 0:NKV * NCMP], w2[:, m_, :], hidc[:, 0, m_, :], start=(m_ == 0), stop=(m_ == 1))
                last.then_inc(q["act_full"], 1)
                b = dve_job("vcmp", l)
                w2 = W(l, "w2v").rearrange("p (a b) -> p a b", a=2)
                for h in range(NKV):
                    for m_ in range(2):
                        last = mm(b[0:NCMP, h * HD:(h + 1) * HD], hidc[:, 1, m_, h * NCMP:(h + 1) * NCMP],
                                  w2[:, m_, :], start=(m_ == 0), stop=(m_ == 1))
                last.then_inc(q["dve_full"], 1)
                b = dve_job("vblk", l)
                wait_drained("vcmp", l)
                rep = C("rep", NCMP).rearrange("p (a b) -> p a b", a=2)
                for h in range(NKV):
                    last = mm(b[0:NH * NCMP, 0:HD], rep[:, h, :], vcmp[:, h, :], start=(h == 0), stop=(h == NKV - 1))
                last.then_inc(q["dve_full"], 1)
                wait_drained("kcmp", l)
                wait_drained("kcat", l, 1)
                wait_drained("vblk", l)
                for t in range(TT):
                    attention(l, t)
                compressed(l, TT - 1)
                mod_cols(l, 4)
                for t in range(TT):
                    b = dve_job("attT", l, t)
                    pe.wait_ge(q["att_n"], n("att_n"))
                    for j in range(D_ATT // P):
                        last = nc.tensor.transpose(b[:, j * P:(j + 1) * P], oatt[t][:, j * P:(j + 1) * P], ident)
                    last.then_inc(q["dve_full"], 1)
                pe.wait_ge(q["y_ready"], n("y_ready", 2))
                wait_drained("attT", l, 1)
                for h in range(2):
                    name = "out" + str(h)
                    arrived(l, name)
                    w = k3(slot_of(l, name)[:, :], KD)
                    for t in range(TT):
                        b = dve_job("out", l, h, t)
                        for k in range(KD):
                            last = mm(b[:, :], yT[:, k, t * P:(t + 1) * P], w[:, k, :],
                                      start=(k == 0), stop=(k == KD - 1))
                        last.then_inc(q["dve_full"], 1)
                    used["head", l, name] = written["out", l, h, TT - 1]
                if l < L - 1:
                    mod_cols(l + 1, 0)
                rows_to_hT(l, 1)
                mod_row(5, l)
                b = dve_job("logits", l)
                w = W(l, "rw").rearrange("p (k n) -> p k n", k=KD)
                for t in range(TT):
                    for k in range(KD):
                        last = mm(b[:, t * NR:(t + 1) * NR], hT[:, k, t * P:(t + 1) * P], w[:, k, :],
                                  start=(k == 0), stop=(k == KD - 1))
                last.then_inc(q["dve_full"], 1)
                b = dve_job("ranks", l)
                pe.wait_ge(q["lg_ready"], n("lg_ready"))
                oh = rt[:, 0:TT * NG].rearrange("p (t g) -> p t g", t=TT)
                mm(b[:, 0:NG], C("tri"), oh[:, 0, :], start=True, stop=True)
                mm(b[:, NG:2 * NG], ones, oh[:, 0, :], start=True, stop=False)
                mm(b[:, NG:2 * NG], C("tri"), oh[:, 1, :], start=False, stop=True)
                mm(b[:, 2 * NG:3 * NG], ones, oh[:, 0, :], start=True, stop=False)
                mm(b[:, 2 * NG:3 * NG], ones, oh[:, 1, :], start=False, stop=True).then_inc(q["dve_full"], 1)

                if l < L - 1:
                    mod_cols(l + 1, 1)
                gather(q, n, l, "first")
                with pe.Fori(0, NG) as g:
                    n.loop(g, TURNS)
                    moe_pass(q, n, l, "loop")
                    n.end(NG)
                n("xg_ready")
                pe.wait_ge(q["routed"], l + 1)
                full = pe.value_load(flag[0:1, 0:1], min_val=0, max_val=1)
                with pe.If(full > 0):
                    n2 = Waits()
                    gather(second[l], n2, l, "second")
                    moe_pass(second[l], n2, l, "second")

        @block.scalar
        def _(act):
            n = Waits()
            A = nc.scalar.activation

            def step(ins):
                return ins.then_inc(q["act_steps"], 1)

            def own():
                act.wait_ge(q["act_steps"], n("act_steps"))

            def full():
                act.wait_ge(q["act_full"], n("act_full"))
                return abank(n("act_jobs"))

            def own_drain():
                act.wait_ge(q["act_free"], n.n["act_jobs"] + 3)

            def evac(dst, src_cols=512, rows=P):
                b = full()
                return A(dst, b[0:rows, 0:src_cols], ACT.Copy).then_inc(q["act_free"], 1)

            def row_roots(tiles_apart=False):
                for t in range(TT):
                    if tiles_apart:
                        act.wait_ge(q["x_done"], n("x_done"))
                    step(A(arena[:, t * D:(t + 1) * D], x[:, t, :], ACT.Square, accum_out=stat[:, t:t + 1]))
                    own()
                    A(stat[:, 2 + t:3 + t], stat[:, t:t + 1], ACT.Sqrt, bias=C("eps"), scale=1.0 / D)\
                        .then_inc(q["norm_root"], 1)

            def rows_to_hT(norm):
                act.wait_ge(q["modcols"], n("modcols"))
                for j in (0, 2):
                    b = full()
                    for i in range(2):
                        k = 2 * j + i
                        last = A(hT[:, k, :], b[:, i * S:(i + 1) * S], ACT.Identity,
                                 bias=cols[:, 2 * norm, k:k + 1], scale=amul[:, norm, k:k + 1])
                    last.then_inc(q["act_free"], 1)

            def split(m, n, l, quarters, wait_chunk):
                for c in quarters:
                    name, i = GROUP[c // 4 % len(GROUP)], c % 4
                    if i == 0:
                        wait_chunk(name, int(c >= QUARTERS))
                    act.wait_ge(m["split_free"], n("split_free"))
                    A(wh[c % NQ][:, :], slot_of(l, name)[:, i * QT:(i + 1) * QT], ACT.Copy)\
                        .then_inc(m["hi_ready"], 1)

            def gather(m, n, l, kind, turn=None, between=lambda: None):
                for ks in GATHER[:-1]:
                    act.wait_ge(m["act_full"], n("act_full"))
                    n("act_jobs")
                    b = abank(n.n["act_jobs"])
                    for i, k in enumerate(ks):
                        last = A(xg[:, k, :], b[:, i * P:(i + 1) * P], ACT.Identity,
                                 bias=cols[:, 2, k:k + 1], scale=amul[:, 1, k:k + 1])
                    last.then_inc(m["act_free"], 1)
                between()
                act.wait_ge(*sem_at(m, drained[kind, l, "gather", 3], turn))
                act.wait_ge(*sem_at(m, drained[kind, l, "gather", 6], turn))
                A(xgh[:, :, :], xg, ACT.Copy).then_inc(m["operand_hi"], 1)

            def moe_pass(m, n, l, kind, turn, wait_chunk, ahead=0):
                next_ = [NQ if kind == "loop" else 0]

                def split_to(end):
                    split(m, n, l, range(next_[0], end), wait_chunk)
                    next_[0] = end

                def gate(e):
                    if e >= 2 or kind == "loop":
                        act.wait_ge(*sem_at(m, drained[kind, l, "u", (e - 2) % NE], turn, int(e < 2)))
                    act.wait_ge(*sem_at(m, written[kind, l, "g", e], turn))
                    n("act_jobs")
                    A(silu[e % 2], bank_of[kind, l, "g", e][:, :], ACT.Silu).then_inc(m["act_free"], 1)

                def hidden(e):
                    act.wait_ge(*sem_at(m, written[kind, l, "hidT", e], turn))
                    A(hidTh[e % 2][:, :], bank_of[kind, l, "hidT", e][:, :], ACT.Copy).then_inc(m["operand_hi"], 1)

                split_to(7)
                gate(0)
                split_to(15)
                gate(1)
                hidden(0)
                split_to(27)
                gate(2)
                hidden(1)
                split_to(39)
                gate(3)
                hidden(2)
                split_to(QUARTERS - 1)
                hidden(3)
                if kind == "loop":
                    gather(m, n, l, kind, turn, lambda: split_to(QUARTERS))
                split_to(QUARTERS + ahead)

            def credits(m):
                act.sem_inc(m["act_free"], 3)

            def split_credits(m):
                act.sem_inc(m["split_free"], NQ)

            credits(q)
            split_credits(q)
            act.wait_ge(q["c_in"], 16)
            A(sc[:, :], scin[:, :], ACT.Silu).then_inc(q["sc_ready"], 1)
            act.wait_ge(q["consts"], 32)
            act.wait_ge(q["x_in"], 16)

            for l in range(L):
                if l:
                    act.wait_ge(q["x_done"], n("x_done"))
                row_roots()
                rows_to_hT(0)
                if l == 0:
                    act.wait_ge(q["angle"], n("angle"))
                    A(sinT[:, :], arena[:, 0:S], ACT.Sin)
                    A(cosT[:, :], arena[:, S:2 * S], ACT.Sin).then_inc(q["trig"], 1)
                    act.wait_ge(q["lam_a"], n("lam_a"))
                    A(ltmp[:, :, 2:4], ltmp[:, :, 0:2], ACT.Exp, scale=-1.0).then_inc(q["lam_e"], 1)
                    act.wait_ge(q["lam_w"], n("lam_w"))
                    A(ltmp[:, :, 8:10], ltmp[:, :, 4:6], ACT.Ln).then_inc(q["lam_ln"], 1)
                evac(cu)
                b = full()
                A(cth, b[:, :], ACT.Tanh, scale=0.5).then_inc(q["act_free"], 1)
                evac(xlp[:, :, LRU_W - 1:])
                b = full()
                A(glg, b[:, :], ACT.Gelu_apprx_tanh).then_inc(q["act_free"], 1)
                evac(raw[:, 0:2, :])
                evac(raw[:, 2:4, :])
                evac(raw[:, 4:6, :])
                evac(vcT, S)
                for i, dst in enumerate((thr, thi)):
                    b = full()
                    for ct in range(2):
                        last = A(dst[:, ct, :], b[:, ct * S:(ct + 1) * S], ACT.Tanh,
                                 bias=lamb[:, l, 2 + 2 * i + ct:3 + 2 * i + ct], scale=0.5)
                    last.then_inc(q["act_free"], 1)
                own_drain()
                for ct in range(2):
                    A(av[:, ct, :], thr[:, ct, :], ACT.Exp, bias=lamb[:, l, ct:ct + 1], scale=lamb[:, l, ct:ct + 1])
                for ct in range(2):
                    last = A(tv[:, ct, :], thr[:, ct, :], ACT.Tanh, bias=lamb[:, l, ct:ct + 1],
                             scale=lamb[:, l, ct:ct + 1])
                last.then_inc(q["lru_at"], 1)
                evac(vslc[:, :, :], TT * P)
                evac(raw[:, 6, :], S)
                evac(vwin[:, :, :], TT * (P + 3 * NH))
                act.dma_start(brow[2], d["ada_b"][l:l + 1, 2 * D:3 * D]).then_inc(q["bias_row"], 16)
                own_drain()
                A(gates[:, :, :, :].rearrange("p t h j -> p t (h j)"), vwin[:, :, P:], ACT.Tanh, scale=0.5)\
                    .then_inc(q["gate_th"], 1)
                act.wait_ge(q["lru_q"], n("lru_q"))
                A(thr, thr, ACT.Sqrt, scale=-1.0).then_inc(q["lru_root"], 1)
                b = full()
                A(crs, b[:, 0:S], ACT.Sqrt, bias=C("eps"), scale=1.0 / D_CONV).then_inc(q["act_free"], 1)
                b = full()
                A(lrs, b[:, 0:S], ACT.Sqrt, bias=C("eps"), scale=1.0 / D_LRU).then_inc(q["act_free"], 1)
                evac(grow[:, 0:CH])
                evac(grow[:, CH:D])
                evac(kcat[:, 0, :, :])
                evac(kcat[:, 1, :, :])
                act.wait_ge(q["conv_ln"], n("conv_ln"))
                for ct in range(2):
                    last = A(cacc[:, ct, :], cacc[:, ct, :], ACT.Silu, bias=W(l, "lnb")[:, ct:ct + 1],
                             scale=W(l, "lng")[:, ct:ct + 1])
                last.then_inc(q["conv_silu"], 1)
                b = full()
                A(crs2, b[:, 0:S], ACT.Sqrt, bias=C("eps"), scale=1.0 / D_CONV).then_inc(q["act_free"], 1)
                for kv in range(2):
                    b = full()
                    lo, hi = 32 * kv, 32 * kv + NKV * NCMP
                    A(hidr[lo:hi, :], b[lo:hi, 0:CMP_HID], ACT.Gelu_apprx_tanh).then_inc(q["act_free"], 1)
                for kv in range(2):
                    b = full()
                    A(hidc[:, kv, :, :], b[:, 0:64].rearrange("p (a c) -> p a c", a=2)[:, :, 0:NKV * NCMP], ACT.Copy)\
                        .then_inc(q["act_free"], 1)
                evac(kcmp[:, :], NKV * NCMP)

                for t in range(TT):
                    w = (t + 1) * P
                    act.wait_ge(q["cmp_s"], n("cmp_s"))
                    A(scmp, scmp, ACT.Exp, scale=HD ** -0.5).then_inc(q["cmp_p"], 1)
                    for i in range(NH // 2 + 1):
                        for h in (2 * i, 2 * i + 1) if i < NH // 2 else ():
                            act.wait_ge(q["s_ready"], n("s_ready"))
                            for ty in range(2):
                                seg = sp[h % 4][:, ty * S:ty * S + w]
                                last = A(seg, seg, ACT.Exp, bias=mx[:, h, 2 + ty:3 + ty],
                                         accum_out=sums[:, t, 1 + ty, h:h + 1])
                            last.then_inc(q["p_ready"], 1)
                        if i == 1:
                            evac(pcT[0:NH * NCMP, :], P, NH * NCMP)
                        if i >= 1:
                            h = (l * TT + t) * NH + 2 * i - 2
                            if h >= 4:
                                act.wait_ge(q["pT_read"], h - 3)
                            evac(pT[h % 4][:, 0:2 * w], 2 * w)
                for t in range(TT):
                    act.wait_ge(q["att_ss"], n("att_ss"))
                    A(astat[:, t, 1:2], astat[:, t, 0:1], ACT.Sqrt, bias=C("eps"), scale=1.0 / D_ATT)\
                        .then_inc(q["att_root"], 1)
                act.dma_start(brow[5], d["ada_b"][l:l + 1, 5 * D:6 * D]).then_inc(q["bias_row"], 16)
                row_roots(tiles_apart=True)
                rows_to_hT(1)
                evac(grow[:, 0:CH])
                evac(grow[:, CH:D])
                def wait_chunk(turn):
                    def wait(name, later):
                        s, before = place(l, name)
                        act.wait_ge(loaded[s], turn * (16 * TURN) + 16 * (before + 1 + later * TURN))
                    return wait

                split(q, n, l, range(NQ), wait_chunk(0))
                act.wait_ge(q["lg_ready"], n("lg_ready"))
                A(rt[:, 60:68], rt[:, 50:58], ACT.Exp).then_inc(q["lg_exp"], 1)
                act.wait_ge(q["top_d"], n("top_d"))
                A(rt[:, 142:144], rt[:, 140:142], ACT.Exp).then_inc(q["top_exp"], 1)

                def wait_chunk2(name, later):
                    j = GROUP.index(name)
                    act.wait_ge(loaded2[l][j % 3], 16 * (j // 3 + 1))

                gather(q, n, l, "first")
                with act.Fori(0, NG - 1) as g:
                    n.loop(g, TURNS)
                    moe_pass(q, n, l, "loop", g, wait_chunk(g), NQ)
                    n.end(NG - 1)
                moe_pass(q, n, l, "loop", NG - 1, wait_chunk(NG - 1))
                act.wait_ge(q["routed"], l + 1)
                more = act.value_load(flag[0:1, 0:1], min_val=0, max_val=1)
                with act.If(more > 0):
                    n2 = Waits()
                    credits(second[l])
                    split_credits(second[l])
                    gather(second[l], n2, l, "second")
                    moe_pass(second[l], n2, l, "second", None, wait_chunk2)

            act.wait_ge(*sem_at(q, written["cols", L - 1, 4]))
            act.dma_start(acc[:, 1, :], d["final_norm_g"]).then_inc(q["gain_in"], 16)
            act.wait_ge(q["x_done"], n("x_done"))
            row_roots()

        @block.vector
        def _(vec):
            n = Waits()
            made = Waits()
            V = nc.vector

            def step(ins, name="dve_steps"):
                made(name)
                return ins.then_inc(q[name], 1)

            def own(name="dve_steps"):
                vec.wait_ge(q[name], made.now(name))

            def do(ins, name="dve_steps"):
                step(ins, name)
                own(name)

            def wait_drained(*key):
                vec.wait_ge(*sem_at(q, drained[key]))

            def full():
                vec.wait_ge(q["dve_full"], n("dve_full"))
                return dbank(n("dve_jobs"))

            def wait(name):
                vec.wait_ge(q[name], n(name))

            def ts(out_, in_, s1, s2, op0, op1=ALU.bypass):
                return V.tensor_scalar(out_, in_, s1, s2, op0, op1)

            def halves(ap):
                return ap.rearrange("p (a b) -> p a b", a=2)

            def modulation(part):
                for h in range(2):
                    name = "ada" + str(2 * part + h)
                    s, before = place(0, name)
                    vec.wait_ge(loaded[s], 16 * (before + 1))
                    w = k3(ring[s][:, :], KD)
                    dst = acc[:, part, h * CH:(h + 1) * CH]
                    do(ts(dst, w[:, 0, :], sc[:, 0:1], None, ALU.mult))
                    for k in range(1, KD):
                        sig = "acc_ready" if h and k == KD - 1 else "dve_steps"
                        do(V.scalar_tensor_tensor(dst, w[:, k, :], sc[:, k:k + 1], dst, ALU.mult, ALU.add), sig)
                    used["head", 0, name] = (sig, made.n[sig])

            def mod_cols(l, col):
                b = full()
                do(V.tensor_tensor(cols[:, col, :], b[:, 0:KD], W(l, "adab")[:, col * KD:(col + 1) * KD], ALU.add), "dve_free")

            def gain_cols(l, norm, name):
                do(V.scalar_tensor_tensor(amul[:, norm, :], cols[:, 2 * norm + 1, :], 1.0, W(l, name),
                                          ALU.add, ALU.mult), "modcols")

            def reciprocal_root(t):
                wait("norm_root")
                do(V.reciprocal(stat[:, 4 + t:5 + t], stat[:, 2 + t:3 + t]))

            def normalize_rows(tiles=range(TT)):
                for t in tiles:
                    reciprocal_root(t)
                    do(ts(xn[:, t, :], x[:, t, :], stat[:, 4 + t:5 + t], None, ALU.mult),
                       "xn_ready" if t == TT - 1 else "dve_steps")

            def rows_to_hT(norm):
                for j in (1, 3):
                    b = full()
                    for i in range(2):
                        k = 2 * j + i
                        step(ts(hT[:, k, :], b[:, i * S:(i + 1) * S], amul[:, norm, k:k + 1],
                                cols[:, 2 * norm, k:k + 1], ALU.mult, ALU.add), "dve_free" if i else "dve_steps")

            def heads(ap):
                return ap.rearrange("p (h e) -> p h e", h=NH)

            def weight(t, j):
                return coef[:, t, j, :].unsqueeze(2).to_broadcast([P, NH, HD])

            def coefficients(l, t):
                vec.wait_ge(q["pT_read"], (l * TT + t + 1) * NH)
                cf = coef[:, t, :, :]
                do(V.reciprocal(cf, sums[:, t, :, :]))
                do(V.tensor_tensor(cf, cf, gates[:, t, :, :].rearrange("p h j -> p j h"), ALU.mult))
                do(ts(coef[:, t, 0, :], coef[:, t, 0, :], C("anyv")[:, t:t + 1], None, ALU.mult))
                b = full()
                do(V.tensor_tensor(heads(oatt[t]), heads(b[:, :]), weight(t, 0), ALU.mult), "dve_free")

            def combine(t):
                for j in range(2):
                    do(V.tensor_tensor(heads(otmp), heads(opsum[j][:, :]), weight(t, 1 + j), ALU.mult),
                       "o_free" if j else "dve_steps")
                    do(V.tensor_tensor(oatt[t], oatt[t], otmp, ALU.add))
                do(V.tensor_tensor_reduce(out=otmp, in0=oatt[t], in1=oatt[t], scale=1.0, scalar=0.0, op0=ALU.mult,
                                          op1=ALU.add, accum_out=astat[:, t, 0:1]), "att_ss")

            def normalize_attention(t):
                wait("att_root")
                do(V.reciprocal(astat[:, t, 2:3], astat[:, t, 1:2]))
                do(ts(oatt[t], oatt[t], astat[:, t, 2:3], None, ALU.mult), "att_n")

            def attention(l, t):
                nb = t + 1
                w = nb * P
                sc3 = scmp.rearrange("p (h n) -> p h n", h=NH)
                mask = C("cmask")[:, t * NCMP:(t + 1) * NCMP]
                for par in range(2):
                    b = full()
                    do(V.tensor_tensor(sc3[:, par::2, :],
                                       b[:, 0:NH * 16].rearrange("p (h n) -> p h n", h=NH)[:, par::2, 0:NCMP],
                                       mask.unsqueeze(1).to_broadcast([P, NH // 2, NCMP]), ALU.add), "dve_free")
                do(V.tensor_reduce(cmx[:, :], sc3, X, ALU.max))
                do(V.tensor_tensor(sc3, sc3, cmx[:, :].unsqueeze(2).to_broadcast([P, NH, NCMP]), ALU.subtract), "cmp_s")
                for i in range(NH // 2 + 1):
                    for j in (2 * i, 2 * i + 1) if i < NH // 2 else ():
                        h = (l * TT + t) * NH + j
                        b = full()
                        if h >= 4:
                            vec.wait_ge(*sem_at(q, written["pT", h - 4]))
                        for ty in range(2):
                            step(V.tensor_tensor_reduce(out=sp[j % 4][:, ty * S:ty * S + w],
                                                         in0=b[:, ty * S:ty * S + w],
                                                         in1=C("causal")[:, 2 * P - w:2 * P], scale=HD ** -0.5,
                                                         scalar=-3e38, op0=ALU.add, op1=ALU.max,
                                                         accum_out=mx[:, j, ty:ty + 1]),
                                 "dve_free" if ty else "dve_steps")
                        own("dve_free")
                        do(ts(mx[:, j, 2:4], mx[:, j, 0:2], -1.0, None, ALU.mult), "s_ready")
                    if i == 0 and t:
                        coefficients(l, t - 1)
                    if i == 1:
                        vec.wait_ge(q["cmp_p"], l * TT + t + 1)
                        do(V.tensor_reduce(sums[:, t, 0, :], sc3, X, ALU.add))
                    if i >= 1:
                        h = (l * TT + t) * NH + 2 * i - 1
                        b = full()
                        if h >= 4:
                            vec.wait_ge(q["pT_read"], h - 3)
                        do(V.tensor_copy(pT[h % 4][:, 0:2 * w], b[:, 0:2 * w]), "dve_free")
                    if i == 1 and t:
                        combine(t - 1)

            gsel, own1 = rt[:, 58:60], rt[:, 158:160]

            def select_tokens():
                do(ts(gcur[:, 1:3], gsel, gcur[:, 0:1], None, ALU.is_equal))
                do(V.tensor_tensor(gcur[:, 3:5], gcur[:, 1:3], own1, ALU.mult))
                for t in range(TT):
                    do(ts(sel[:, t, :], C("iota"), gcur[:, 3 + t:4 + t], None, ALU.is_equal),
                       "sel_ready" if t == TT - 1 else "dve_steps")

            def maker(m, n, made):
                def full():
                    vec.wait_ge(m["dve_full"], n("dve_full"))
                    n("dve_jobs")
                    return dbank(n.n["dve_jobs"])

                def step(ins, name="dve_steps"):
                    made(name)
                    return ins.then_inc(m[name], 1)

                def do(ins, name="dve_steps"):
                    step(ins, name)
                    vec.wait_ge(m[name], made.now(name))

                return full, step, do

            def rest(m, n, made, l, quarters, kind):
                for c in quarters:
                    name, i = GROUP[c // 4 % len(GROUP)], c % 4
                    vec.wait_ge(m["hi_ready"], n("hi_ready"))
                    made("lo_ready")
                    V.tensor_tensor(wl[c % NQ][:, :], slot_of(l, name)[:, i * QT:(i + 1) * QT], wh[c % NQ][:, :],
                                    ALU.subtract).then_inc(m["lo_ready"], 1)
                    if i == 3 and (kind == "second" or n.turn is not None):
                        used[kind, l, name] = ("lo_ready", made.n["lo_ready"])

            def gather(m, n, made, l, kind, between=lambda: None):
                full, step, do = maker(m, n, made)
                b = full()
                for i, k in enumerate(GATHER[-1]):
                    step(ts(xg[:, k, :], b[:, i * P:(i + 1) * P], amul[:, 1, k:k + 1], cols[:, 2, k:k + 1],
                            ALU.mult, ALU.add), "dve_free" if i else "dve_steps")
                between()
                vec.wait_ge(m["operand_hi"], n("operand_hi"))
                step(V.tensor_tensor(xgl[:, :, :], xg, xgh[:, :, :], ALU.subtract), "xg_ready")

            def moe_pass(m, n, made, l, kind, turn, ahead=0):
                full, step, do = maker(m, n, made)
                next_ = [NQ if kind == "loop" else 0]

                def rest_to(end):
                    rest(m, n, made, l, range(next_[0], end), kind)
                    next_[0] = end

                def hidden(e):
                    vec.wait_ge(*sem_at(m, drained[kind, l, "g", e], turn))
                    vec.wait_ge(*sem_at(m, written[kind, l, "u", e], turn))
                    n("dve_jobs")
                    b = bank_of[kind, l, "u", e]
                    if e >= 2 or kind == "loop":
                        vec.wait_ge(*sem_at(m, written[kind, l, "hidT", (e - 2) % NE], turn, int(e < 2)))
                    step(V.scalar_tensor_tensor(hid[e % 2], b[:, :], wslot[:, e:e + 1], silu[e % 2],
                                                ALU.mult, ALU.mult), "dve_free")

                def hidden_rest(e):
                    b = full()
                    vec.wait_ge(m["operand_hi"], n("operand_hi"))
                    step(V.tensor_tensor(hidTl[e % 2][:, :], b[:, :], hidTh[e % 2][:, :], ALU.subtract), "dve_free")

                rest_to(7)
                b = full()
                step(V.tensor_copy(wslot[:, :], b[:, 0:NE]), "dve_free")
                b = full()
                step(V.tensor_copy(selT[:, :, :], b[:, 0:TT * P].rearrange("p (a b) -> p a b", a=2)), "dve_free")
                vec.wait_ge(m["dve_free"], made.now("dve_free"))
                rest_to(11)
                hidden(0)
                rest_to(15)
                hidden_rest(0)
                rest_to(19)
                hidden(1)
                if kind == "loop":
                    do(ts(gcur[:, 0:1], gcur[:, 0:1], 1.0, None, ALU.add))
                    do(ts(gcur[:, 1:3], gsel, gcur[:, 0:1], None, ALU.is_equal))
                    do(V.tensor_tensor(gcur[:, 3:5], gcur[:, 1:3], own1, ALU.mult))
                    for t in range(TT):
                        step(ts(sel[:, t, :], C("iota"), gcur[:, 3 + t:4 + t], None, ALU.is_equal),
                             "sel_ready" if t == TT - 1 else "dve_steps")
                rest_to(27)
                hidden_rest(1)
                rest_to(31)
                hidden(2)
                rest_to(39)
                hidden_rest(2)
                rest_to(43)
                hidden(3)
                rest_to(QUARTERS - 1)
                hidden_rest(3)
                if kind == "loop":
                    gather(m, n, made, l, kind, between=lambda: rest_to(QUARTERS))
                rest_to(QUARTERS + min(1, ahead))
                vec.wait_ge(*sem_at(m, written[kind, l, "d", NE - 1], turn))
                for h in range(2):
                    step(V.tensor_tensor(ys[:, h * CH:(h + 1) * CH], opsum[h][:, :],
                                         grow[:, h * CH:(h + 1) * CH], ALU.mult), "ys_ready")
                rest_to(QUARTERS + ahead)
                for h in range(2):
                    for t in range(TT):
                        b = full()
                        dst = x[:, t, h * CH:(h + 1) * CH]
                        step(V.tensor_tensor(dst, b[:, :], dst, ALU.add), "dve_free")
                vec.wait_ge(m["dve_free"], made.now("dve_free"))

            def credits(m):
                vec.sem_inc(m["dve_free"], 3)

            def tables():
                vec.wait_ge(q["late_in"], 16 * L)
                MAGIC, PI = 1.5 * 2.0 ** 23, 3.1415925
                C1 = 6.28125
                C2 = float(np.float32(np.float64(2 * np.pi) - C1).view(np.uint32).__and__(0xFFFFF000).astype(np.uint32)
                           .view(np.float32))
                C3 = float(2 * np.pi - C1 - C2)
                ang, rnd, r2 = arena[:, 0:S], arena[:, 2 * S:3 * S], arena[:, S:2 * S]
                do(V.tensor_copy(r2, posi[:, :]))
                do(ts(ang, r2, C("inv"), None, ALU.mult))
                do(ts(rnd, ang, 1.0 / (2 * np.pi), MAGIC, ALU.mult, ALU.add))
                do(ts(rnd, rnd, MAGIC, None, ALU.subtract))
                for part in (C1, C2, C3):
                    do(V.scalar_tensor_tensor(ang, rnd, -part, ang, ALU.mult, ALU.add))
                do(ts(ang, ang, PI, -PI, ALU.min, ALU.max))
                do(ts(r2, ang, np.pi / 2, None, ALU.add))
                do(ts(rnd, r2, PI, -2 * np.pi, ALU.is_gt, ALU.mult))
                do(V.tensor_tensor(r2, r2, rnd, ALU.add))
                do(ts(r2, r2, PI, -PI, ALU.min, ALU.max), "angle")
                for l in range(L):
                    do(V.scalar_tensor_tensor(ltmp[:, l, 0:2], W(l, "lam"), -1.0, W(l, "lam"), ALU.mult, ALU.max), "lam_a" if l == L - 1 else "dve_steps")
                wait("lam_e")
                le, lw_, ld, ll, lz = (ltmp[:, :, i:i + 2] for i in (2, 4, 6, 8, 10))
                do(ts(lw_, le, 1.0, None, ALU.add))
                do(ts(ld, lw_, 1.0, None, ALU.subtract), "lam_w")
                do(ts(lz, ld, 0.0, None, ALU.is_equal))
                wait("lam_ln")
                do(V.tensor_tensor(ll, ll, lz, ALU.add))
                do(V.tensor_tensor(ld, ld, lz, ALU.add))
                do(V.reciprocal(ld, ld))
                do(V.tensor_tensor(ll, ll, ld, ALU.mult))
                do(V.tensor_tensor(ll, ll, le, ALU.mult))
                for l in range(L):
                    do(ts(ltmp[:, l, 4:6], W(l, "lam"), -1.0, 0.0, ALU.mult, ALU.max))
                    do(V.tensor_tensor(ltmp[:, l, 4:6], ltmp[:, l, 4:6], ltmp[:, l, 8:10], ALU.add))
                    do(ts(lamb[:, l, 0:2], ltmp[:, l, 4:6], -4.0, None, ALU.mult))
                    do(ts(lamb[:, l, 2:4], W(l, "ba"), 0.5, None, ALU.mult))
                    do(ts(lamb[:, l, 4:6], W(l, "bx"), 0.5, None, ALU.mult))

            credits(q)
            made("dve_free", 3)
            step(V.memset(xlp[:, :, 0:LRU_W - 1], 0.0))
            wait("sc_ready")
            modulation(0)
            modulation(1)
            vec.wait_ge(q["consts"], 32)
            normalize_rows()
            mod_cols(0, 0)
            mod_cols(0, 1)
            gain_cols(0, 0, "n1g")

            for l in range(L):
                if l:
                    normalize_rows()
                rows_to_hT(0)
                if l == 0:
                    tables()
                do(V.memset(vp[:, :, 0:CONV_K - 1], 0.0))
                wait_drained("conv", l, 1)
                do(ts(csq, cth, 0.5, 0.5, ALU.mult, ALU.add))
                do(V.tensor_tensor(vp[:, :, CONV_K - 1:], cu, csq, ALU.mult))
                cw = W(l, "ccw").rearrange("p (a b) -> p a b", a=2)
                for j in range(CONV_K):
                    for ct in range(2):
                        if j:
                            vec.wait_ge(q["dve_steps"], made.now("dve_steps") - 1 + (j == CONV_K - 1 and ct))
                            step(V.scalar_tensor_tensor(cacc[:, ct, :], vp[:, ct, j:j + S], cw[:, ct, j:j + 1],
                                                        cacc[:, ct, :], ALU.mult, ALU.add),
                                 "conv_sum" if j == CONV_K - 1 and ct else "dve_steps")
                        else:
                            step(ts(cacc[:, ct, :], vp[:, ct, 0:S], cw[:, ct, 0:1], W(l, "ccb")[:, ct:ct + 1],
                                    ALU.mult, ALU.add))
                own("conv_sum")
                wait_drained("lru", l, 0)
                lw4 = W(l, "lcw").rearrange("p (a b) -> p a b", a=2)
                for j in range(LRU_W):
                    for ct in range(2):
                        if j:
                            do(V.scalar_tensor_tensor(xc[:, ct, :], xlp[:, ct, j:j + S], lw4[:, ct, j:j + 1],
                                                      xc[:, ct, :], ALU.mult, ALU.add),
                               "lru_conv" if ct and j == LRU_W - 1 else "dve_steps")
                        else:
                            do(ts(xc[:, ct, :], xlp[:, ct, 0:S], lw4[:, ct, 0:1], W(l, "lcb")[:, ct:ct + 1],
                                  ALU.mult, ALU.add))
                b = full()
                for ct in range(2):
                    do(V.scalar_tensor_tensor(cacc[:, ct, :], b[:, 0:S], -1.0 / D_CONV, cacc[:, ct, :],
                                              ALU.mult, ALU.add), "dve_free" if ct else "dve_steps")
                do(V.tensor_tensor(csq, cacc[:, :, :], cacc[:, :, :], ALU.mult), "conv_sq")
                wait("lru_at")
                do(V.tensor_tensor(thr, av, av, ALU.mult))
                do(V.scalar_tensor_tensor(thr, thr, 1.0, tv, ALU.add, ALU.mult), "lru_q")
                do(ts(thi, thi, 0.5, 0.5, ALU.mult, ALU.add))
                do(V.tensor_tensor(thi, thi, xc, ALU.mult))
                wait("lru_root")
                do(V.tensor_tensor(thi, thi, thr, ALU.mult))
                for ct in range(2):
                    do(V.tensor_tensor_scan(xc[:, ct, :], av[:, ct, :], thi[:, ct, :], 0.0, ALU.mult, ALU.add))
                do(V.tensor_tensor(xc, xc, glg, ALU.mult))
                do(V.tensor_tensor(thr, xc, xc, ALU.mult), "lru_sq")
                if l == 0:
                    wait("trig")
                for lo, hi in ((0, 2), (2, 4), (4, 6), (6, 7)):
                    w = hi - lo
                    b = full()
                    pa = ropa[:, 0:w * S].rearrange("p (a b) -> p a b", a=w)
                    pb = ropb[:, 0:w * S].rearrange("p (a b) -> p a b", a=w)
                    step(V.tensor_tensor(pa, b[:, 0:w * S].rearrange("p (a b) -> p a b", a=w),
                                         sinT[:, :].unsqueeze(1).to_broadcast([P, w, S]), ALU.mult), "dve_free")
                    do(V.tensor_tensor(pb, raw[:, lo:hi, :], cosT[:, :].unsqueeze(1).to_broadcast([P, w, S]),
                                       ALU.mult))
                    do(V.tensor_tensor(raw[:, lo:hi, :], pa, pb, ALU.add), "rope_ready" if hi == 7 else "dve_steps")
                wait_drained("conv_sd", l)
                do(V.reciprocal(crs, crs))
                do(V.tensor_tensor(cacc[:, :, :], cacc[:, :, :], crs.unsqueeze(1).to_broadcast([P, 2, S]),
                                   ALU.mult), "conv_ln")
                gn = W(l, "gn")
                wait_drained("lru_rms", l)
                do(V.reciprocal(lrs, lrs))
                for ct in range(2):
                    do(V.scalar_tensor_tensor(yT[:, ct, :], xc[:, ct, :], gn[:, ct:ct + 1], lrs,
                                              ALU.mult, ALU.mult), "y_ready" if ct else "dve_steps")
                for h in range(NKV):
                    b = full()
                    for kv in range(2):
                        src = b[:, kv * S:(kv + 1) * S].rearrange("p (m s r) -> p m s r", s=CMP_STRIDE // 2, r=2)
                        pos = W(l, "posk" if kv == 0 else "posv")
                        for r in range(2):
                            lo, hi = r * HD, (r + 1) * HD
                            for a in range(2):
                                step(V.tensor_tensor(
                                    blkG[lo:hi, kv, 8 * a:8 * a + 8, h, :],
                                    src[lo:hi, a:a + NCMP, :, r].rearrange("p n s -> p s n"),
                                    pos[lo:hi, 8 * a:8 * a + 8].unsqueeze(2).to_broadcast([HD, 8, NCMP]), ALU.add),
                                     "dve_free" if kv and r and a else "dve_steps")
                mod_cols(l, 2)
                wait("conv_silu")
                do(V.tensor_tensor(csq, cacc[:, :, :], cacc[:, :, :], ALU.mult), "conv_sq2")
                wait("gate_th")
                do(ts(gates[:, :, :, :], gates[:, :, :, :], 0.5, 0.5, ALU.mult, ALU.add))
                wait_drained("conv_rms", l)
                do(V.reciprocal(crs2, crs2))
                for ct in range(2):
                    do(V.scalar_tensor_tensor(yT[:, 6 + ct, :], cacc[:, ct, :], gn[:, 6 + ct:7 + ct], crs2,
                                              ALU.mult, ALU.mult), "y_ready" if ct else "dve_steps")
                b = full()
                do(V.tensor_copy(vcmp[:, :, :], b[0:NCMP, 0:NKV * HD].rearrange("p (a b) -> p a b", a=NKV)),
                   "dve_free")
                b = full()
                R = NH * NCMP
                do(V.tensor_tensor(vblk[:, :, :], b[0:R, 0:HD].unsqueeze(1).to_broadcast([R, NH, HD]),
                                   C("blk", R).unsqueeze(2).to_broadcast([R, NH, HD]), ALU.mult), "dve_free")

                for t in range(TT):
                    attention(l, t)
                coefficients(l, TT - 1)
                for t in range(TT - 1):
                    normalize_attention(t)
                combine(TT - 1)
                mod_cols(l, 3)
                gain_cols(l, 1, "n2g")
                normalize_attention(TT - 1)
                for t in range(TT):
                    b = full()
                    do(V.tensor_tensor(yT[:, 2:6, t * P:(t + 1) * P], b[:, :].rearrange("p (a b) -> p a b", a=4),
                                       gn[:, 2:6].unsqueeze(2).to_broadcast([P, 4, P]), ALU.mult), "dve_free")
                wait_drained("row", l, 2, 1)
                for h in range(2):
                    for t in range(TT):
                        b = full()
                        dst = x[:, t, h * CH:(h + 1) * CH]
                        do(V.tensor_tensor(ropa, b[:, :], grow[:, h * CH:(h + 1) * CH], ALU.mult), "dve_free")
                        do(V.tensor_tensor(dst, dst, ropa, ALU.add), "x_done" if h else "dve_steps")
                        if h and t < TT - 1:
                            normalize_rows([t])
                if l < L - 1:
                    mod_cols(l + 1, 0)
                normalize_rows([TT - 1])
                rows_to_hT(1)

                def tg(lo):
                    return rt[:, lo:lo + TT * NG].rearrange("p (t g) -> p t g", t=TT)

                def tv2(lo):
                    return rt[:, lo:lo + TT]

                def bc(ap):
                    return ap.unsqueeze(2).to_broadcast([P, TT, NG])

                def row4(name):
                    return C(name).unsqueeze(1).to_broadcast([P, TT, NG])

                def first_max(scores, top, onehot, scratch, index):
                    do(V.tensor_reduce(top, scores, X, ALU.max))
                    do(V.tensor_tensor(scratch, scores, bc(top), ALU.is_ge))
                    do(V.scalar_tensor_tensor(scratch, scratch, -1000.0, row4("gfar"), ALU.mult, ALU.add))
                    do(V.tensor_reduce(index, scratch, X, ALU.min))
                    do(V.tensor_tensor(onehot, row4("gidx"), bc(index), ALU.is_equal))

                lg = rt[:, 8:8 + TT * NR].rearrange("p (t n) -> p t n", t=TT)
                b = full()
                do(V.tensor_tensor(lg, b[:, 0:TT * NR].rearrange("p (t n) -> p t n", t=TT),
                                   W(l, "rb").unsqueeze(1).to_broadcast([P, TT, NR]), ALU.add), "dve_free")
                first_max(lg[:, :, 0:NG], tv2(48), tg(0), tg(50), gsel)
                do(V.tensor_tensor(tg(50), lg[:, :, 0:NG], bc(tv2(48)), ALU.subtract))
                do(V.tensor_copy(tg(180), tg(0)), "lg_ready")
                prod = rt[:, 80:112].rearrange("p (t g e) -> p t g e", t=TT, g=NG)
                for t in range(TT):
                    do(V.tensor_tensor(prod[:, t, :, :], lg[:, t, NG:].rearrange("p (g e) -> p g e", g=NG),
                                       tg(0)[:, t, :].unsqueeze(2).to_broadcast([P, NG, NE]), ALU.mult))
                    do(V.tensor_reduce(tg(72)[:, t, :], prod[:, t, :, :].rearrange("p g e -> p e g"), X, ALU.add))
                first_max(tg(72), tv2(112), tg(114), tg(188), tv2(196))
                do(V.scalar_tensor_tensor(tg(122), tg(114), NEG, tg(72), ALU.mult, ALU.add))
                first_max(tg(122), tv2(130), tg(132), tg(188), tv2(196))
                do(V.tensor_tensor(tv2(140), tv2(130), tv2(112), ALU.subtract), "top_d")
                b = full()
                do(V.tensor_tensor(tg(150), b[:, 0:2 * NG].rearrange("p (t g) -> p t g", t=TT), tg(0), ALU.mult))
                do(V.tensor_reduce(own1, tg(150), X, ALU.add))
                do(ts(own1, own1, 1.0, None, ALU.add))
                do(V.memset(gcur[:, 0:1], 0.0))
                do(ts(rt[:, 164:168], b[:, 2 * NG:3 * NG], float(P), None, ALU.is_gt), "dve_free")
                select_tokens()
                if l < L - 1:
                    mod_cols(l + 1, 1)
                do(V.tensor_reduce(rt[:, 168:169], rt[:, 164:168], X, ALU.max))
                do(V.tensor_tensor(rt[:, 160:164], rt[:, 164:168], C("gidx"), ALU.mult))
                do(V.tensor_reduce(rt[:, 169:170], rt[:, 160:164], X, ALU.add))
                do(V.tensor_copy(flag[:, :], rt[0:1, 168:170]), "routed")
                wait("lg_exp")
                do(V.tensor_reduce(tv2(68), tg(60), X, ALU.add))
                do(V.reciprocal(tv2(170), tv2(68)))
                wait("top_exp")
                do(ts(tv2(144), tv2(142), 1.0, None, ALU.add))
                do(V.reciprocal(tv2(146), tv2(144)))
                do(V.tensor_tensor(tv2(148), tv2(142), tv2(146), ALU.mult))
                do(V.tensor_tensor(tg(114), tg(114), bc(tv2(146)), ALU.mult))
                do(V.tensor_tensor(tg(132), tg(132), bc(tv2(148)), ALU.mult))
                do(V.tensor_tensor(tg(114), tg(114), tg(132), ALU.add))
                do(V.tensor_tensor(we[:, :, :], tg(114), bc(tv2(170)), ALU.mult))
                wait_drained("row", l, 5, 1)
                if l < L - 1:
                    gain_cols(l + 1, 0, "n1g")

                rest(q, n, made, l, range(NQ), None)
                gather(q, n, made, l, "first")
                with vec.Fori(0, NG - 1) as g:
                    n.loop(g, TURNS)
                    made.loop(g, TURNS)
                    moe_pass(q, n, made, l, "loop", g, NQ)
                    n.end(NG - 1)
                    made.end(NG - 1)
                moe_pass(q, n, made, l, "loop", NG - 1)
                more = vec.value_load(flag[0:1, 0:1], min_val=0, max_val=1)
                with vec.If(more > 0):
                    m2, made2 = second[l], Waits()
                    credits(m2)
                    made2("dve_free", 3)

                    def do2(ins, name="dve_steps"):
                        ins.then_inc(m2[name], 1)
                        vec.wait_ge(m2[name], made2(name))

                    do2(V.tensor_copy(gcur[:, 0:1], rt[:, 169:170]))
                    do2(ts(own1, own1, -float(P), None, ALU.add))
                    do2(ts(gcur[:, 1:3], gsel, gcur[:, 0:1], None, ALU.is_equal))
                    do2(V.tensor_tensor(gcur[:, 3:5], gcur[:, 1:3], own1, ALU.mult))
                    for t in range(TT):
                        do2(ts(sel[:, t, :], C("iota"), gcur[:, 3 + t:4 + t], None, ALU.is_equal),
                            "sel_ready" if t == TT - 1 else "dve_steps")
                    n2 = Waits()
                    gather(m2, n2, made2, l, "second")
                    moe_pass(m2, n2, made2, l, "second", None)
                do(V.memset(gcur[:, 0:1], 0.0), "x_done")

            vec.wait_ge(q["gain_in"], 16)
            for t in range(TT):
                reciprocal_root(t)
                do(V.scalar_tensor_tensor(xn[:, t, :], x[:, t, :], stat[:, 4 + t:5 + t], acc[:, 1, :],
                                          ALU.mult, ALU.mult), "out_ready")

        @block.gpsimd
        def _(pool):
            made = Waits()
            made("acc_ready", 2)

            def do(ins, name="pool_steps"):
                ins.then_inc(q[name], 1)
                pool.wait_ge(q[name], made(name))

            def modulation(l, part, names, last_use):
                pool.wait_ge(*last_use)
                for h, (ring_l, name) in enumerate(names):
                    s, before = place(ring_l, name)
                    pool.wait_ge(loaded[s], 16 * (before + 1))
                    w = k3(ring[s][:, :], KD)
                    add = nc.gpsimd.tensor_tensor
                    do(add(w, w, sc[:, :].unsqueeze(2).to_broadcast([P, KD, CH]), ALU.mult))
                    do(add(w[:, 0:4, :], w[:, 0:4, :], w[:, 4:8, :], ALU.add))
                    do(add(w[:, 0:2, :], w[:, 0:2, :], w[:, 2:4, :], ALU.add))
                    sig = "acc_ready" if h else "pool_steps"
                    do(add(acc[:, (6 * l + part) % 3, h * CH:(h + 1) * CH], w[:, 0, :], w[:, 1, :], ALU.add), sig)
                    used["head", ring_l, name] = (sig, made.n[sig])

            pool.wait_ge(q["sc_ready"], 1)
            for l in range(L):
                for part in range(2, 6):
                    last_use = {2: ("acc_read", 2 * l), 3: written["cols", l, 0], 4: written["cols", l, 1],
                                5: ("acc_read", 2 * l + 1)}[part]
                    if part == 2 and l == 0:
                        last_use = ("sc_ready", 1)
                    modulation(l, part, [(l, "ada" + str(2 * part + h)) for h in range(2)], sem_at(q, last_use))
                if l < L - 1:
                    for part in range(2):
                        modulation(l + 1, part, [(l, "next" + str(2 * part + h)) for h in range(2)],
                                   sem_at(q, written["cols", l, 3 + part]))

        @block.sync
        def _(sync):
            def source(l, name):
                kind = name.rstrip("0123456789")
                if kind == "next":
                    l, kind, name = l + 1, "ada", "ada" + name[4:]
                if kind == "ada":
                    c = CH * int(name[3:])
                    return d["ada_w"][l].rearrange("(p k) n -> p k n", k=KD)[:, :, c:c + CH]
                if kind == "cmpk" or kind == "cmpv":
                    w1 = d["cmp_k_w1"] if kind == "cmpk" else d["cmp_v_w1"]
                    return w1[l].rearrange("(k p) n -> p k n", p=P)
                if kind == "out":
                    c = CH * int(name[3:])
                    return d["w_out"][l].rearrange("(k p) n -> p k n", p=P)[:, :, c:c + CH]
                lo, hi = {"conv": C_CONV, "lru": C_LRU, "q": C_Q, "kv": C_KV, "win": C_WIN}[kind]
                return d["w_in"][l].rearrange("(p k) n -> p k n", k=KD)[:, :, lo:hi]

            def load(l, name):
                s = place(l, name)[0]
                src = source(l, name)
                k, w = src.shape[1], src.shape[2]
                sync.dma_start(k3(ring[s][:, 0:k * w], k), src).then_inc(loaded[s], 16)

            def load_expert(l, name, g, sem):
                src = EX[name[0]][bass.ds(g * NE + (l * NG * NE + int(name[1])), 1), :, :]
                sync.dma_start(ring[place(l, name)[0]][:, :], src.rearrange("a p n -> p (a n)")).then_inc(sem, 16)

            sync.dma_start(scin[:, :], d["c"]).then_inc(q["c_in"], 16)
            load(0, "ada0")
            load(0, "ada1")
            sync.dma_start(const[:, :], d["consts"]).then_inc(q["consts"], 16)
            sync.dma_start(x[:, :, :], d["x"].rearrange("a (t p) n -> p (a t) n", p=P)).then_inc(q["x_in"], 16)
            load(0, "ada2")
            load(0, "ada3")
            sync.dma_start(param[0][:, :], d["params"][0]).then_inc(q["consts"], 16)
            sync.dma_start(posi[:, :], d["positions"]).then_inc(q["late_in"], 16)
            for l in range(1, L):
                sync.dma_start(param[l][:, :], d["params"][l]).then_inc(q["late_in"], 16)
            first, rest = GROUP[:NSLOT], GROUP[NSLOT:]
            for l in range(L):
                head = HEADS[l]
                for i, name in enumerate(head):
                    if l == 0 and i < 4:
                        continue
                    if i >= NSLOT:
                        sync.wait_ge(*sem_at(q, used["head", l, head[i - NSLOT]]))
                    elif l:
                        sync.wait_ge(*sem_at(q, used["loop", l - 1, GROUP[i - NSLOT]], NG - 1))
                    load(l, name)
                for i, name in enumerate(first):
                    sync.wait_ge(*sem_at(q, used["head", l, head[i - NSLOT]]))
                    load_expert(l, name, 0, loaded[place(l, name)[0]])
                with sync.Fori(0, NG - 1) as g:
                    for name, last in zip(rest, GROUP):
                        sync.wait_ge(*sem_at(q, used["loop", l, last], g))
                        load_expert(l, name, g, loaded[place(l, name)[0]])
                    for name, last in zip(first, GROUP[-NSLOT:]):
                        sync.wait_ge(*sem_at(q, used["loop", l, last], g))
                        load_expert(l, name, g + 1, loaded[place(l, name)[0]])
                for name, last in zip(rest, GROUP):
                    sync.wait_ge(*sem_at(q, used["loop", l, last], NG - 1))
                    load_expert(l, name, NG - 1, loaded[place(l, name)[0]])
                sync.wait_ge(q["routed"], l + 1)
                full = sync.value_load(flag[0:1, 0:1], min_val=0, max_val=1)
                with sync.If(full > 0):
                    g2 = sync.value_load(flag[0:1, 1:2], min_val=0, max_val=NG - 1)
                    for name in GROUP[-NSLOT:]:
                        sync.wait_ge(*sem_at(q, used["loop", l, name], NG - 1))
                    for j, name in enumerate(GROUP):
                        if j >= 3:
                            sync.wait_ge(*sem_at(second[l], used["second", l, GROUP[j - 3]]))
                        load_expert(l, name, g2, loaded2[l][j % 3])
                    for name in GROUP[-3:]:
                        sync.wait_ge(*sem_at(second[l], used["second", l, name]))
            for t in range(TT):
                sync.wait_ge(q["out_ready"], t + 1)
                sync.dma_start(out[0, t * P:(t + 1) * P, :], xn[:, t, :]).then_inc(q["stored"], 16)
            sync.wait_ge(q["stored"], 16 * TT)


INS = ("moe_w_gate", "moe_w_up", "moe_w_down", "ada_w", "ada_b", "w_in", "w_out", "cmp_k_w1", "cmp_v_w1", "x")


def kernel(**inputs):
    import concourse.bacc as bacc
    from concourse.bass_utils import run_bass_kernel_spmd

    a = {k: np.ascontiguousarray(v) for k, v in inputs.items()}
    nc = bacc.Bacc("TRN2", target_bir_lowering=False, num_devices=1)

    def dcol(v):
        return v.reshape(P, KD)

    def ccol(v):
        return v.reshape(-1, P).T

    params = np.zeros((L, P, NPARAM), np.float32)
    for l in range(L):
        def put(name, v):
            lo, hi = PARAM[name]
            params[l, :, lo:hi] = v.reshape(P, hi - lo)

        put("n1g", dcol(a["norm1_g"][l]))
        put("n2g", dcol(a["norm2_g"][l]))
        put("adab", np.concatenate([dcol(a["ada_b"][l, i * D:(i + 1) * D]) for i in (0, 1, 3, 4)], 1))
        put("lcw", a["lru_conv_w"][l].reshape(LRU_W, 2, P).transpose(2, 1, 0))
        put("lcb", ccol(a["lru_conv_b"][l]))
        put("ba", ccol(a["lru_ba"][l]))
        put("bx", ccol(a["lru_bx"][l]))
        put("lam", ccol(a["lru_lambda"][l]))
        put("ccw", a["cnv_dw_w"][l].reshape(CONV_K, 2, P).transpose(2, 1, 0))
        put("ccb", ccol(a["cnv_dw_b"][l]))
        put("lng", ccol(a["cnv_ln_g"][l]))
        put("lnb", ccol(a["cnv_ln_b"][l]))
        put("gn", ccol(a["out_norm_g"][l]))
        rb = np.concatenate([a["moe_rg_b"][l], a["moe_re_b"][l].reshape(-1)])
        put("rb", np.broadcast_to(rb, (P, NR)))
        for name, src in (("posk", "cmp_pos_k"), ("posv", "cmp_pos_v")):
            put(name, a[src][l].reshape(LP, P).T)
        for name, src in (("wa", "lru_wa"), ("wx", "lru_wx")):
            w = np.zeros((P, 2, P), np.float32)
            for i in range(4):
                o = 64 * (i % 2)
                w[o:o + 64, i // 2, o:o + 64] = a[src][l, i]
            put(name, w)
        rw = np.concatenate([a["moe_rg_w"][l], a["moe_re_w"][l].transpose(1, 0, 2).reshape(D, NG * NE)], 1)
        put("rw", rw)
        w2 = a["cmp_k_w2"][l].reshape(2, P, HD).transpose(1, 0, 2)
        put("w2k", np.concatenate([w2, w2], 2))
        put("w2v", a["cmp_v_w2"][l].reshape(2, P, HD).transpose(1, 0, 2))

    arrays = {k: a[k] for k in INS}
    arrays["params"] = params
    arrays["consts"] = constants()
    arrays["c"] = dcol(a["c"][0])
    arrays["positions"] = np.ascontiguousarray(np.broadcast_to(a["positions"], (P, S)))
    arrays["final_norm_g"] = np.ascontiguousarray(np.broadcast_to(a["final_norm_g"], (P, D)))
    d = {}
    feeds = {}
    for name, v in arrays.items():
        v = np.ascontiguousarray(v)
        feeds[name + "_in"] = v
        d[name] = nc.dram_tensor(name + "_in", v.shape, mybir.dt.from_np(v.dtype), kind="ExternalInput").ap()
    out = nc.dram_tensor("out", (1, S, D), mybir.dt.float32, kind="ExternalOutput").ap()
    build(nc, d, out)
    r = run_bass_kernel_spmd(nc, [feeds], core_ids=[0])
    return r.results[0]["out"]
```
